# Optimizing a Trainium2 kernel written in Bass

```python
import math
import jax, jax.numpy as jnp
from jax import lax
import numpy as np

D_MODEL = 1024
BATCH = 1
SEQ = 256
DEPTH = 1

CHUNK = 64
A_HEADS = 8
A_DK = 128
A_DV = 128
A_CONV = 4
A_W = A_HEADS * A_DV
B_HEADS = 16
B_DH = 64
B_W = B_HEADS * B_DH
B_PREV_CHUNKS = 8
B_MAX_REL = 256
B_REL_SIZE = CHUNK - 1 + B_MAX_REL + 1
D_FF = 2816
FFN_CONV = 3
N_BRANCHES = 2
IN_SPLITS = (3 * A_W, 4 * A_W, 4 * A_W + A_HEADS, 4 * A_W + 2 * A_HEADS,
             4 * A_W + 2 * A_HEADS + B_W, 4 * A_W + 2 * A_HEADS + 2 * B_W,
             4 * A_W + 2 * A_HEADS + 3 * B_W)
IN_COLS = 4 * A_W + 2 * A_HEADS + 3 * B_W + N_BRANCHES * D_MODEL
DEEPNORM_ALPHA = (2.0 * DEPTH) ** 0.25
DEEPNORM_BETA = (8.0 * DEPTH) ** -0.25
LN_EPS = 1e-5
RMS_EPS = 1e-6
L2_EPS = 1e-6
NEG_INF = -1e30


def layernorm(x, g, b):
    xf = x.astype(jnp.float32)
    mu = jnp.mean(xf, axis=-1, keepdims=True)
    var = jnp.mean(jnp.square(xf - mu), axis=-1, keepdims=True)
    y = (xf - mu) * lax.rsqrt(var + LN_EPS) * g.astype(jnp.float32) + b.astype(jnp.float32)
    return y.astype(x.dtype)

def causal_dwconv(x, w):
    k_width, ch = w.shape
    return lax.conv_general_dilated(
        x, w[:, None, :].astype(x.dtype), window_strides=(1,), padding=[(k_width - 1, 0)],
        dimension_numbers=("NWC", "WIO", "NWC"), feature_group_count=ch)

def l2norm(x):
    return x * lax.rsqrt(jnp.sum(jnp.square(x), axis=-1, keepdims=True) + L2_EPS)

def chunk_gated_delta_rule(q, k, v, g, beta):
    b_, s_, h_, dk = q.shape
    dv = v.shape[-1]
    n_chunks = s_ // CHUNK

    def to_chunks(t):
        return t.reshape(b_, n_chunks, CHUNK, h_, -1).transpose(0, 1, 3, 2, 4)

    q, k, v = to_chunks(q), to_chunks(k), to_chunks(v)
    g = g.reshape(b_, n_chunks, CHUNK, h_).transpose(0, 1, 3, 2)
    beta = beta.reshape(b_, n_chunks, CHUNK, h_).transpose(0, 1, 3, 2)
    g = jnp.cumsum(g, axis=-1)

    causal = jnp.tril(jnp.ones((CHUNK, CHUNK), dtype=bool))
    strict = jnp.tril(jnp.ones((CHUNK, CHUNK), dtype=bool), k=-1)
    diff = g[..., :, None] - g[..., None, :]
    decay = jnp.where(causal, jnp.exp(jnp.where(causal, diff, 0.0)), 0.0)

    k_beta = k * beta[..., None]
    v_beta = v * beta[..., None]
    a_low = jnp.where(strict, jnp.einsum("bnhid,bnhjd->bnhij", k_beta, k) * decay, 0.0)
    eye = jnp.eye(CHUNK, dtype=jnp.float32)
    rhs = jnp.concatenate([v_beta, k_beta * jnp.exp(g)[..., None]], axis=-1)
    sol = lax.linalg.triangular_solve(a_low + eye, rhs, left_side=True, lower=True,
                                      unit_diagonal=True)
    u = sol[..., :dv]
    w = sol[..., dv:]
    qk = jnp.where(causal, jnp.einsum("bnhid,bnhjd->bnhij", q, k) * decay, 0.0)

    def step(state, inp):
        q_n, k_n, u_n, w_n, qk_n, g_n = inp
        v_new = u_n - jnp.einsum("bhck,bhkv->bhcv", w_n, state)
        o_n = (jnp.einsum("bhck,bhkv->bhcv", q_n * jnp.exp(g_n)[..., None], state)
               + jnp.einsum("bhij,bhjv->bhiv", qk_n, v_new))
        g_last = g_n[..., -1]
        k_dec = k_n * jnp.exp(g_last[..., None] - g_n)[..., None]
        state = state * jnp.exp(g_last)[..., None, None] + jnp.einsum("bhck,bhcv->bhkv", k_dec, v_new)
        return state, o_n

    xs = tuple(jnp.moveaxis(t, 1, 0) for t in (q, k, u, w, qk, g))
    state0 = jnp.zeros((b_, h_, dk, dv), jnp.float32)
    _, o = lax.scan(step, state0, xs)
    return o.transpose(1, 0, 3, 2, 4).reshape(b_, s_, h_, dv)

def gated_deltanet(qkv, z, beta_raw, a_raw, conv_w, a_log, dt_bias, norm_w):
    b_, s_, _ = qkv.shape
    qkv = jax.nn.silu(causal_dwconv(qkv, conv_w))
    q, k, v = jnp.split(qkv.astype(jnp.float32), 3, axis=-1)
    q = l2norm(q.reshape(b_, s_, A_HEADS, A_DK)) * (A_DK ** -0.5)
    k = l2norm(k.reshape(b_, s_, A_HEADS, A_DK))
    v = v.reshape(b_, s_, A_HEADS, A_DV)
    beta = jax.nn.sigmoid(beta_raw.astype(jnp.float32))
    g = -jnp.exp(a_log.astype(jnp.float32)) * jax.nn.softplus(
        a_raw.astype(jnp.float32) + dt_bias.astype(jnp.float32))
    o = chunk_gated_delta_rule(q, k, v, g, beta)
    o = o * lax.rsqrt(jnp.mean(jnp.square(o), axis=-1, keepdims=True) + RMS_EPS)
    o = o * norm_w.astype(jnp.float32) * jax.nn.silu(z.astype(jnp.float32).reshape(b_, s_, A_HEADS, A_DV))
    return o.reshape(b_, s_, A_W).astype(qkv.dtype)

def chunk_band_attention(q, k, v, rel_bias):
    b_, s_, h_, dh = q.shape
    n_chunks = s_ // CHUNK
    pad = B_PREV_CHUNKS * CHUNK
    band = (B_PREV_CHUNKS + 1) * CHUNK
    k_pad = jnp.pad(k, ((0, 0), (pad, 0), (0, 0), (0, 0)))
    v_pad = jnp.pad(v, ((0, 0), (pad, 0), (0, 0), (0, 0)))
    qi = np.arange(CHUNK)[:, None]
    kj = np.arange(band)[None, :]
    dist = pad + qi - kj
    idx = np.clip(dist, -(CHUNK - 1), B_MAX_REL) + (CHUNK - 1)
    bias = rel_bias.astype(jnp.float32)[:, idx]
    key_chunk = jnp.arange(band) // CHUNK
    scale = dh ** -0.5

    def one_chunk(n):
        q_n = lax.dynamic_slice_in_dim(q, n * CHUNK, CHUNK, axis=1)
        k_n = lax.dynamic_slice_in_dim(k_pad, n * CHUNK, band, axis=1)
        v_n = lax.dynamic_slice_in_dim(v_pad, n * CHUNK, band, axis=1)
        valid = (n - B_PREV_CHUNKS + key_chunk) >= 0
        s = jnp.einsum("bqhd,bkhd->bhqk", q_n, k_n).astype(jnp.float32) * scale + bias
        s = jnp.where(valid, s, NEG_INF)
        p = jax.nn.softmax(s, axis=-1).astype(v.dtype)
        return jnp.einsum("bhqk,bkhd->bqhd", p, v_n)

    out = lax.map(one_chunk, jnp.arange(n_chunks))
    return out.transpose(1, 0, 2, 3, 4).reshape(b_, s_, h_ * dh)

def first_inputs(seed: int = 0) -> dict:
    key = jax.random.key(seed)
    ks = jax.random.split(key, 24)

    def nrm(k, shape, scale):
        return jax.random.normal(k, shape, jnp.float32) * scale

    L = DEPTH
    x = nrm(ks[0], (BATCH, SEQ, D_MODEL), 1.0)
    c = nrm(ks[1], (BATCH, D_MODEL), 1.0)
    w_ada = nrm(ks[2], (L, D_MODEL, 6 * D_MODEL), D_MODEL ** -0.5)
    b_ada = nrm(ks[3], (L, 6 * D_MODEL), 0.02)
    w_in = nrm(ks[4], (L, D_MODEL, IN_COLS), D_MODEL ** -0.5)
    b_gate = nrm(ks[5], (L, N_BRANCHES * D_MODEL), 0.1)
    conv_a = nrm(ks[6], (L, A_CONV, 3 * A_W), A_CONV ** -0.5)
    a_log = jnp.log(jax.random.uniform(ks[7], (L, A_HEADS), jnp.float32, minval=1.0, maxval=16.0))
    dt = jnp.exp(jax.random.uniform(ks[8], (L, A_HEADS), jnp.float32,
                                    minval=math.log(1e-3), maxval=math.log(1e-1)))
    dt_bias = dt + jnp.log(-jnp.expm1(-dt))
    norm_a = 1.0 + nrm(ks[9], (L, A_DV), 0.05)
    rel_bias = nrm(ks[10], (L, B_HEADS, B_REL_SIZE), 0.2)
    w_branch_a = nrm(ks[11], (L, A_W, D_MODEL), A_W ** -0.5)
    w_branch_b = nrm(ks[12], (L, B_W, D_MODEL), B_W ** -0.5)
    w_o = nrm(ks[13], (L, D_MODEL, D_MODEL), DEEPNORM_BETA * D_MODEL ** -0.5)
    ln1_g = 1.0 + nrm(ks[14], (L, D_MODEL), 0.05)
    ln1_b = nrm(ks[15], (L, D_MODEL), 0.02)
    w_up = nrm(ks[16], (L, D_MODEL, 2 * D_FF), D_MODEL ** -0.5)
    conv_ffn = nrm(ks[17], (L, FFN_CONV, 2 * D_FF), FFN_CONV ** -0.5)
    b_conv_ffn = nrm(ks[18], (L, 2 * D_FF), 0.02)
    w_down = nrm(ks[19], (L, D_FF, D_MODEL), DEEPNORM_BETA * D_FF ** -0.5)
    ln2_g = 1.0 + nrm(ks[20], (L, D_MODEL), 0.05)
    ln2_b = nrm(ks[21], (L, D_MODEL), 0.02)
    return {"x": x, "c": c, "w_ada": w_ada, "b_ada": b_ada, "w_in": w_in, "b_gate": b_gate,
            "conv_a": conv_a, "a_log": a_log, "dt_bias": dt_bias, "norm_a": norm_a,
            "rel_bias": rel_bias, "w_branch_a": w_branch_a, "w_branch_b": w_branch_b, "w_o": w_o,
            "ln1_g": ln1_g, "ln1_b": ln1_b, "w_up": w_up, "conv_ffn": conv_ffn,
            "b_conv_ffn": b_conv_ffn, "w_down": w_down, "ln2_g": ln2_g, "ln2_b": ln2_b}

def first_block(x, c, w_ada, b_ada, w_in, b_gate, conv_a, a_log, dt_bias, norm_a, rel_bias,
              w_branch_a, w_branch_b, w_o, ln1_g, ln1_b, w_up, conv_ffn, b_conv_ffn, w_down,
              ln2_g, ln2_b):
    b_, s_, d_ = x.shape
    c_act = jax.nn.silu(c)
    for l in range(DEPTH):
        mod = (c_act @ w_ada[l] + b_ada[l])[:, None, :]
        shift_t, scale_t, gate_t, shift_f, scale_f, gate_f = jnp.split(mod, 6, axis=-1)

        h = x * (1.0 + scale_t) + shift_t
        proj = h @ w_in[l]
        qkv_a, z_a, beta_raw, a_raw, q_b, k_b, v_b, gates = jnp.split(proj, IN_SPLITS, axis=-1)

        o_a = gated_deltanet(qkv_a, z_a, beta_raw, a_raw, conv_a[l], a_log[l], dt_bias[l], norm_a[l])
        o_b = chunk_band_attention(q_b.reshape(b_, s_, B_HEADS, B_DH),
                                   k_b.reshape(b_, s_, B_HEADS, B_DH),
                                   v_b.reshape(b_, s_, B_HEADS, B_DH), rel_bias[l])

        gate_a, gate_b = jnp.split(jax.nn.sigmoid(gates + b_gate[l]), N_BRANCHES, axis=-1)
        merged = gate_a * (o_a @ w_branch_a[l]) + gate_b * (o_b @ w_branch_b[l])
        mix = merged @ w_o[l]
        x = layernorm(DEEPNORM_ALPHA * x + gate_t * mix, ln1_g[l], ln1_b[l])

        h = x * (1.0 + scale_f) + shift_f
        u = causal_dwconv(h @ w_up[l], conv_ffn[l]) + b_conv_ffn[l]
        u_gate, u_val = jnp.split(u, 2, axis=-1)
        ffn = (jax.nn.silu(u_gate) * u_val) @ w_down[l]
        x = layernorm(DEEPNORM_ALPHA * x + gate_f * ffn, ln2_g[l], ln2_b[l])
    return x


DEPTH_2 = 2

N_META = 16
EPS = 1e-6
GLA_HEADS = 4
GLA_DV = D_MODEL // 2 // GLA_HEADS
GLA_DK = GLA_DV // 2
GLA_LOWRANK = 16
GLA_TAU = 16.0
FOX_DH = 64
FOX_HEADS = D_MODEL // 2 // FOX_DH
Q_BLOCK = 128
FORGET_BIAS_INIT = 4.0
D_FF_2 = 128 * (-(-8 * D_MODEL // (3 * 128)))
CONV_W = 3
GLA_WIDTH = GLA_HEADS * GLA_DV
FOX_WIDTH = FOX_HEADS * FOX_DH
MIX_WIDTH = GLA_WIDTH + FOX_WIDTH
IN_SIZES = (GLA_HEADS * GLA_DK, GLA_HEADS * GLA_DK, GLA_WIDTH, GLA_WIDTH, GLA_LOWRANK,
            FOX_WIDTH, FOX_WIDTH, FOX_WIDTH, FOX_HEADS)
N_IN = sum(IN_SIZES)


def rms_norm(x, g):
    xf = x.astype(jnp.float32)
    y = xf * lax.rsqrt(jnp.mean(xf * xf, axis=-1, keepdims=True) + EPS)
    return (y * g.astype(jnp.float32)).astype(x.dtype)

def chunk_kv_summary(k, v, log_a):
    log_b = jnp.cumsum(log_a, axis=3)
    log_end = log_b[:, :, :, -1:, :]
    u = jnp.einsum('bhntk,bhntv->bhnkv', k * jnp.exp(log_end - log_b), v)
    return u, jnp.exp(log_end[:, :, :, 0, :])

def gla_chunk_causal(q, k, v, log_a):
    B, L, H, _ = q.shape
    dv = v.shape[-1]
    n_chunks = (L - N_META) // CHUNK

    def split(t):
        t = jnp.transpose(t.astype(jnp.float32), (0, 2, 1, 3))
        d = t.shape[-1]
        return (t[:, :, :N_META].reshape(B, H, 1, N_META, d),
                t[:, :, N_META:].reshape(B, H, n_chunks, CHUNK, d))

    q_m, q_r = split(q)
    k_m, k_r = split(k)
    v_m, v_r = split(v)
    a_m, a_r = split(log_a)
    u_m, _ = chunk_kv_summary(k_m, v_m, a_m)
    s_meta = u_m[:, :, 0]
    u_r, decay_r = chunk_kv_summary(k_r, v_r, a_r)

    def step(s, inp):
        u_c, d_c = inp
        s = d_c[..., None] * s + u_c
        return s, s

    _, states = lax.scan(step, s_meta, (jnp.moveaxis(u_r, 2, 0), jnp.moveaxis(decay_r, 2, 0)))
    states = jnp.moveaxis(states, 0, 2)
    o_m = jnp.einsum('bhtk,bhkv->bhtv', q_m[:, :, 0], s_meta)
    o_r = jnp.einsum('bhntk,bhnkv->bhntv', q_r, states).reshape(B, H, n_chunks * CHUNK, dv)
    o = jnp.concatenate([o_m, o_r], axis=2)
    return jnp.transpose(o, (0, 2, 1, 3))

def forgetting_attention(q, k, v, log_f):
    B, L, H, dh = q.shape
    n_blk = -(-L // Q_BLOCK)
    pad = n_blk * Q_BLOCK - L
    c = jnp.cumsum(log_f.astype(jnp.float32), axis=1)
    c_k = jnp.transpose(c, (0, 2, 1))
    c_q = jnp.pad(c, ((0, 0), (0, pad), (0, 0)), mode='edge')
    q_pad = jnp.pad(q.astype(jnp.float32) * dh ** -0.5, ((0, 0), (0, pad), (0, 0), (0, 0)))
    q_blocks = jnp.moveaxis(q_pad.reshape(B, n_blk, Q_BLOCK, H, dh), 1, 0)
    c_blocks = jnp.moveaxis(jnp.transpose(c_q.reshape(B, n_blk, Q_BLOCK, H), (0, 1, 3, 2)), 1, 0)
    kf = k.astype(jnp.float32)
    vf = v.astype(jnp.float32)
    key_pos = jnp.arange(L)

    def block(inp):
        q_b, c_b, start = inp
        logits = (jnp.einsum('bqhd,bkhd->bhqk', q_b, kf)
                  + c_b[..., None] - c_k[:, :, None, :])
        q_pos = start + jnp.arange(Q_BLOCK)
        logits = jnp.where(key_pos[None, :] <= q_pos[:, None], logits, -jnp.inf)
        return jnp.einsum('bhqk,bkhd->bqhd', jax.nn.softmax(logits, axis=-1), vf)

    out = lax.map(block, (q_blocks, c_blocks, jnp.arange(n_blk) * Q_BLOCK))
    out = jnp.moveaxis(out, 0, 1).reshape(B, n_blk * Q_BLOCK, H, dh)
    return out[:, :L]

def conv_ffn(x, w_up, conv_w, conv_b, w_down):
    h = x @ w_up
    L = h.shape[1]
    hp = jnp.pad(h, ((0, 0), (CONV_W - 1, 0), (0, 0)))
    hc = conv_b
    for j in range(CONV_W):
        hc = hc + hp[:, j:j + L] * conv_w[j]
    u, g = jnp.split(hc, 2, axis=-1)
    return (jax.nn.silu(g) * u) @ w_down

def second_inputs(seed: int = 0) -> dict:
    key = jax.random.key(seed)
    ks = jax.random.split(key, 16)

    def nrm(k, shape, scale):
        return jax.random.normal(k, shape, jnp.float32) * scale

    return {
        'x': nrm(ks[0], (BATCH, SEQ, D_MODEL), 1.0),
        'meta_tokens': nrm(ks[1], (N_META, D_MODEL), 1.0),
        'attn_norm': 1.0 + nrm(ks[2], (DEPTH_2, D_MODEL), 0.02),
        'w_in': nrm(ks[3], (DEPTH_2, D_MODEL, N_IN), D_MODEL ** -0.5),
        'w_alpha_up': nrm(ks[4], (DEPTH_2, GLA_LOWRANK, GLA_HEADS * GLA_DK), GLA_LOWRANK ** -0.5),
        'b_alpha': nrm(ks[5], (DEPTH_2, GLA_HEADS * GLA_DK), 0.1),
        'b_forget': FORGET_BIAS_INIT + nrm(ks[6], (DEPTH_2, FOX_HEADS), 0.5),
        'gla_norm': 1.0 + nrm(ks[7], (DEPTH_2, GLA_WIDTH), 0.02),
        'fox_norm': 1.0 + nrm(ks[8], (DEPTH_2, FOX_WIDTH), 0.02),
        'w_out': nrm(ks[9], (DEPTH_2, MIX_WIDTH, D_MODEL), MIX_WIDTH ** -0.5),
        'ffn_norm': 1.0 + nrm(ks[10], (DEPTH_2, D_MODEL), 0.02),
        'w_up': nrm(ks[11], (DEPTH_2, D_MODEL, 2 * D_FF_2), D_MODEL ** -0.5),
        'conv_w': nrm(ks[12], (DEPTH_2, CONV_W, 2 * D_FF_2), CONV_W ** -0.5),
        'conv_b': nrm(ks[13], (DEPTH_2, 2 * D_FF_2), 0.02),
        'w_down': nrm(ks[14], (DEPTH_2, D_FF_2, D_MODEL), D_FF_2 ** -0.5),
        'final_norm': 1.0 + nrm(ks[15], (D_MODEL,), 0.02),
    }

def second_block(x, meta_tokens, attn_norm, w_in, w_alpha_up, b_alpha, b_forget, gla_norm,
              fox_norm, w_out, ffn_norm, w_up, conv_w, conv_b, w_down, final_norm):
    B = x.shape[0]
    meta = jnp.broadcast_to(meta_tokens[None].astype(x.dtype), (B, N_META, D_MODEL))
    h = jnp.concatenate([meta, x], axis=1)
    L = h.shape[1]
    cuts = np.cumsum(IN_SIZES)[:-1].tolist()
    for i in range(DEPTH_2):
        xn = rms_norm(h, attn_norm[i])
        gq, gk, gv, gr, glr, fq, fk, fv, ff = jnp.split(xn @ w_in[i], cuts, axis=-1)
        log_a = jax.nn.log_sigmoid((glr @ w_alpha_up[i] + b_alpha[i]).astype(jnp.float32)) / GLA_TAU
        o_gla = gla_chunk_causal(gq.reshape(B, L, GLA_HEADS, GLA_DK) * GLA_DK ** -0.5,
                                 gk.reshape(B, L, GLA_HEADS, GLA_DK),
                                 gv.reshape(B, L, GLA_HEADS, GLA_DV),
                                 log_a.reshape(B, L, GLA_HEADS, GLA_DK)).astype(h.dtype)
        o_gla = rms_norm(o_gla, gla_norm[i].reshape(GLA_HEADS, GLA_DV)).reshape(B, L, GLA_WIDTH)
        o_gla = o_gla * jax.nn.silu(gr)
        log_f = jax.nn.log_sigmoid((ff + b_forget[i]).astype(jnp.float32))
        o_fox = forgetting_attention(fq.reshape(B, L, FOX_HEADS, FOX_DH),
                                     fk.reshape(B, L, FOX_HEADS, FOX_DH),
                                     fv.reshape(B, L, FOX_HEADS, FOX_DH), log_f).astype(h.dtype)
        o_fox = rms_norm(o_fox, fox_norm[i].reshape(FOX_HEADS, FOX_DH)).reshape(B, L, FOX_WIDTH)
        h = h + jnp.concatenate([o_gla, o_fox], axis=-1) @ w_out[i]
        h = h + conv_ffn(rms_norm(h, ffn_norm[i]), w_up[i], conv_w[i], conv_b[i], w_down[i])
    return rms_norm(h, final_norm)[:, N_META:]


def setup_inputs(seed=0):
    out = dict(first_inputs(seed))
    for name, value in second_inputs(seed + 1).items():
        if name != "x":
            out[name + "_2"] = value
    return out


def reference(
    x, c, w_ada, b_ada, w_in, b_gate, conv_a, a_log, dt_bias, norm_a, rel_bias, w_branch_a,
    w_branch_b, w_o, ln1_g, ln1_b, w_up, conv_ffn, b_conv_ffn, w_down, ln2_g, ln2_b,
    meta_tokens_2, attn_norm_2, w_in_2, w_alpha_up_2, b_alpha_2, b_forget_2, gla_norm_2,
    fox_norm_2, w_out_2, ffn_norm_2, w_up_2, conv_w_2, conv_b_2, w_down_2, final_norm_2,
):
    x = first_block(
        x, c, w_ada, b_ada, w_in, b_gate, conv_a, a_log, dt_bias, norm_a, rel_bias, w_branch_a,
        w_branch_b, w_o, ln1_g, ln1_b, w_up, conv_ffn, b_conv_ffn, w_down, ln2_g, ln2_b,
    )
    return second_block(
        x, meta_tokens_2, attn_norm_2, w_in_2, w_alpha_up_2, b_alpha_2, b_forget_2, gla_norm_2,
        fox_norm_2, w_out_2, ffn_norm_2, w_up_2, conv_w_2, conv_b_2, w_down_2, final_norm_2,
    )


_drawn_inputs = setup_inputs


def setup_inputs(seed=0):
    import zlib

    import numpy as np

    out = dict(_drawn_inputs(seed))
    spreads = {}
    factors = {'b_gate': 3.38,
     'norm_a': 3.176,
     'rel_bias': 4.51,
     'b_conv_ffn': 3.298,
     'gla_norm_2': 5.919,
     'fox_norm_2': 2.999,
     'ffn_norm_2': 3.242,
     'conv_b_2': 3.182,
     'final_norm_2': 2.865}
    for name, (base, spread) in spreads.items():
        noise = np.random.default_rng([zlib.crc32(name.encode()), seed]).standard_normal(out[name].shape)
        drawn = base * np.exp(spread * noise) if base else spread * noise
        out[name] = __import__('jax').numpy.asarray(drawn.astype(out[name].dtype))
    for name, factor in factors.items():
        out[name] = (out[name] * factor).astype(out[name].dtype)
    return out
```

```python
from contextlib import ExitStack

import numpy as np
import concourse.bass as bass
from concourse import mybir

F32 = mybir.dt.float32
F32R = mybir.dt.float32r
ALU = mybir.AluOpType
ACT = mybir.ActivationFunctionType
AX_X = mybir.AxisListType.X

P = 128
D = 1024
KD = D // P
SEQ = 256
META = 16
LEN2 = META + SEQ
CH = 64
A_HEADS, A_DK, A_CONV = 8, 128, 4
B_HEADS, B_DH = 16, 64
B_REL = 320
D_FF = 2816
KF = D_FF // P
NG = 3
ALPHA = 2.0 ** 0.25
LN_EPS, RMS_EPS, L2_EPS = 1e-5, 1e-6, 1e-6
LAYERS = 2
GLA_HEADS, GLA_DK, GLA_DV, GLA_LOW, GLA_TAU = 4, 64, 128, 16, 16.0
FOX_HEADS, FOX_DH = 8, 64
NEG = -1e30
TOK2 = [(0, META), (META, P), (META + P, P)]

_PRM = [("c", KD), ("b_ada", 6 * KD), ("b_gate", 2 * KD), ("conv_a", A_CONV * 24), ("norm_a", 1),
        ("ln1_g", KD), ("ln1_b", KD), ("ln2_g", KD), ("ln2_b", KD), ("conv_f", 3 * 2 * KF), ("b_conv_f", 2 * KF)]
for _l in range(LAYERS):
    _PRM += [(f"attn_norm{_l}", KD), (f"b_alpha{_l}", 2), (f"gla_norm{_l}", 4), (f"fox_norm{_l}", 4),
             (f"ffn_norm{_l}", KD), (f"conv_w{_l}", 3 * 2 * KF), (f"conv_b{_l}", 2 * KF)]
_PRM += [("final_norm", KD)]
PRM, NPRM = {}, 0
for _name, _n in _PRM:
    PRM[_name] = NPRM
    NPRM += _n

_CST = [("ident", P), ("flip", P), ("ones", LEN2), ("mask_low", P), ("mask_up", P), ("levels", 6 * P), ("halves", P),
        ("fox_mask", LEN2), ("restart_gla", LEN2), ("restart", SEQ)]
CST, NCST = {}, 0
for _name, _n in _CST:
    CST[_name] = NCST
    NCST += _n


def constants():
    i, j = np.arange(P)[:, None], np.arange(P)[None, :]
    same = (i // CH) == (j // CH)
    levels = []
    for l in range(6):
        b = 1 << l
        levels.append(((i // (2 * b)) == (j // (2 * b))) & ((i // b) % 2 == 1) & ((j // b) % 2 == 0))
    k = np.arange(LEN2)[None, :]
    out = np.zeros((P, NCST), np.float32)

    def put(name, a):
        out[:, CST[name]:CST[name] + a.shape[1]] = a

    put("ident", np.eye(P))
    put("flip", np.eye(P)[::-1])
    put("ones", np.ones((P, LEN2)))
    put("mask_low", np.where(same & (j <= i), 0.0, NEG))
    put("mask_up", np.where(same & (i <= j), 0.0, NEG))
    put("levels", np.concatenate(levels, axis=1))
    put("halves", same)
    put("fox_mask", np.where(k - TOK2[2][0] <= i, 0.0, NEG))
    put("restart_gla", np.broadcast_to(~((k == 0) | ((k >= META) & ((k - META) % CH == 0))), (P, LEN2)))
    put("restart", np.broadcast_to(np.arange(SEQ)[None, :] % CH != 0, (P, SEQ)))
    return out


class Queue:

    def __init__(self, sem, serial):
        self.serial = serial
        self.sem, self.count, self.steps, self.seen = sem, 0, [], {}

    def wait(self, tokens):
        for sem, value in tokens:
            if value > self.seen.get(id(sem), 0):
                self.seen[id(sem)] = value
                self.steps.append(lambda e, s=sem, v=value: e.wait_ge(s, v))

    def run(self, after, *fns, loose=False):
        self.wait(after)
        if self.serial and not loose and self.count:
            self.wait([(self.sem, self.count)])
        for fn in fns[:-1]:
            self.steps.append(fn)
        self.count += 1
        self.steps.append(lambda e, f=fns[-1]: f(e).then_inc(self.sem, 1))
        return (self.sem, self.count)

    def play(self, engine):
        for step in self.steps:
            step(engine)


class Bank:

    def __init__(self, ap):
        self.ap, self.free = ap, []


class Banks:
    def __init__(self, aps):
        self.all, self.at = [Bank(a) for a in aps], -1

    def take(self):
        for _ in self.all:
            self.at = (self.at + 1) % len(self.all)
            b = self.all[self.at]
            if b.free is not None:
                free, b.free = b.free, None
                return b, free
        raise RuntimeError("all banks are held")


class Split:

    def __init__(self, hi, lo, base=0):
        self.hi, self.lo, self.base = hi, lo, base
        self.ready, self.read = [[] for _ in range(KD)], []


def two_blocks(nc, ins, out):
    ctx = ExitStack()
    with ctx:
        def sb(name, cols, dt=F32):
            return ctx.enter_context(nc.sbuf_tensor(name, [P, cols], dt))

        def sem(name):
            return ctx.enter_context(nc.semaphore(name))

        pe, sp = (Queue(sem(n), False) for n in ("pe_done", "sp_done"))
        act, dve = (Queue(sem(n), True) for n in ("act_done", "dve_done"))

        NRAW, NUNIT = 3, 3
        raw = sb("raw_weights", NRAW * 4096)
        whi = sb("weights_hi", NUNIT * 1024, F32R)
        wlo = sb("weights_lo", NUNIT * 1024, F32R)
        hin_hi = sb("hin_hi", KD * LEN2, F32R)
        hin_lo = sb("hin_lo", KD * LEN2, F32R)
        u_hi = sb("u_hi", KD * LEN2, F32R)
        u_lo = sb("u_lo", KD * LEN2, F32R)
        xt = sb("residual", KD * LEN2)
        cst = sb("constants", NCST)
        prm = sb("parameters", NPRM)
        prm8 = sb("head_parameters", 4)
        walpha = sb("w_alpha", LAYERS * 2 * P)
        mod = sb("modulation", 6 * KD)
        cact = sb("c_act", KD)
        small = sb("small", 256)
        NFA = 19712
        arena = sb("arena", NFA)

        def t3(x, n, w=LEN2):
            return x[:, 0:n * w].rearrange("p (k t) -> p k t", t=w)

        X3 = t3(xt, KD)
        HIN = Split(t3(hin_hi, KD), t3(hin_lo, KD))
        U = Split(t3(u_hi, KD), t3(u_lo, KD))
        Xs = X3[:, :, META:LEN2]

        def C(name, n=None, rows=P, at=0):
            a = CST[name] + at
            return cst[0:rows, a:a + (n or P)]

        def prm_col(name, i, rows=P):
            a = PRM[name] + i
            return prm[0:rows, a:a + 1]

        acc_banks = Banks([ctx.enter_context(nc.psum_tensor(f"acc{i}", [P, 512], F32)) for i in range(3)])
        banks = Banks([ctx.enter_context(nc.psum_tensor(f"part{i}", [P, 512], F32)) for i in range(5)])

        def mm(o, l, r, start=True, stop=True):
            return lambda e: e.matmul(o, l, r, start=start, stop=stop)

        def tr(o, i, rows):
            return lambda e: e.transpose(o, i, C("ident", rows, rows=rows))

        def tt(after, o, a, b, op):
            return dve.run(after, lambda e: e.tensor_tensor(o, a, b, op))

        def ts(after, o, a, s1, op0, s2=None, op1=None):
            if op1 is None:
                return dve.run(after, lambda e: e.tensor_scalar(o, a, s1, None, op0))
            return dve.run(after, lambda e: e.tensor_scalar(o, a, s1, s2, op0, op1))

        def stt(after, o, a, s, b, op0, op1):
            return dve.run(after, lambda e: e.scalar_tensor_tensor(out=o, in0=a, scalar=s, in1=b, op0=op0, op1=op1))

        def fn(after, o, i, f, **kw):
            return act.run(after, lambda e: e.activation(o, i, f, **kw))

        def bc(ap, n):
            return ap.unsqueeze(1).broadcast_to([ap.shape[0], n, ap.shape[1]])

        def bci(ap, n):
            return ap.unsqueeze(2).broadcast_to([ap.shape[0], ap.shape[1], n])

        s_small = sem("small_loaded")
        loads = [
            (Xs, ins["x"].rearrange("p (k t) -> p k t", t=SEQ)),
            (prm[:, :], ins["params"]), (cst[:, :], ins["consts"]),
            (prm8[0:8, :], ins["params8"]),
            (X3[:, :, 0:META], ins["meta"].rearrange("p (k t) -> p k t", t=META)),
            (walpha[0:GLA_LOW, :].rearrange("p (l n) -> p l n", l=LAYERS), ins["w_alpha_up_2"].rearrange("l p n -> p l n")),
        ]

        def load(dst, src, s, after=()):
            sp.wait(after)
            sp.steps.append(lambda e: e.dma_start(dst, src).then_inc(s, 16))

        for dst, src in loads:
            load(dst, src, s_small)
        SMALL = (s_small, 16 * len(loads))

        raw_sem = [sem(f"raw{i}_loaded") for i in range(NRAW)]
        chunks = []
        units = []
        loaded = [0]

        chunk_read = {}

        def load_chunks():
            while loaded[0] < len(chunks) and (loaded[0] < NRAW or loaded[0] - NRAW in chunk_read):
                c = loaded[0]
                loaded[0] += 1
                load(chunk_ap(c), chunks[c][0], raw_sem[c % NRAW], chunk_read.get(c - NRAW, []))

        def chunk_ap(c):
            src, nk, w = chunks[c]
            r = c % NRAW
            return raw[:, r * 4096:r * 4096 + nk * w].rearrange("p (k n) -> p k n", n=w)

        def chunk_ready(c):
            return (raw_sem[c % NRAW], 16 * (c // NRAW + 1))

        def weights(w, rows, cols, x, T, evac, tag):
            (r0, r1), (c0, c1) = rows, cols
            n0 = 0
            for a in range(c0, c1, 512):
                width = min(512, c1 - a)
                nk = (r1 - r0) // P
                chunks.append((w[r0:r1, a:a + width].rearrange("(k p) n -> p k n", p=P), nk, width))
                for j in range(width // P):
                    units.append(dict(chunk=len(chunks) - 1, col=j, nk=nk, x=x, T=T, evac=evac, n=n0,
                                      last=j == width // P - 1, tag=tag))
                    n0 += 1

        def modulation(j):
            w = ins["w_ada"]
            chunks.append((w[:, 512 * j:512 * (j + 1)].rearrange("(k p) n -> p k n", p=P), KD, 512))
            units.append(dict(chunk=len(chunks) - 1, ada=j, tag="ada"))

        split_of, taken = {}, [0]
        pe_of_unit = {}

        def split_unit(i):
            if i >= len(units) or i in split_of or "ada" in units[i]:
                return
            un = units[i]
            slot = un["slot"]
            src = chunk_ap(un["chunk"])[:, :, un["col"] * P:(un["col"] + 1) * P]
            n = un["nk"] * P
            hi = whi[:, slot * 1024:slot * 1024 + n].rearrange("p (k n) -> p k n", n=P)
            lo = wlo[:, slot * 1024:slot * 1024 + n].rearrange("p (k n) -> p k n", n=P)
            free = [pe_of_unit[un["before"]]] if un["before"] is not None else []
            h = act.run([chunk_ready(un["chunk"])] + free, lambda e: e.copy(hi, src), loose=True)
            l = dve.run([chunk_ready(un["chunk"]), h] + free,
                        lambda e: e.tensor_tensor(lo, src, hi.bitcast(F32), ALU.subtract), loose=True)
            split_of[i] = (hi, lo, h, l)
            if un["last"]:
                chunk_read[un["chunk"]] = [h, l]
                load_chunks()

        def number_units():
            seen = []
            for i, un in enumerate(units):
                if "ada" in un:
                    continue
                un["slot"] = len(seen) % NUNIT
                un["before"] = seen[len(seen) - NUNIT] if len(seen) >= NUNIT else None
                seen.append(i)

        def step():
            i = taken[0]
            taken[0] += 1
            un = units[i]
            for a in range(i, i + NUNIT):
                if a < len(units) and "ada" not in units[a] and (units[a]["before"] is None or units[a]["before"] < i):
                    split_unit(a)
            if "ada" in un:
                c, j = un["chunk"], un["ada"]
                w = chunk_ap(c)
                b, free = banks.take()
                t = pe.run([chunk_ready(c), CACT] + free,
                           *[mm(b.ap[:, m:m + 1], w[:, k, m * P:(m + 1) * P], cact[:, k:k + 1], k == 0, k == KD - 1)
                             for m in range(4) for k in range(KD)])
                chunk_read[c] = [t]
                load_chunks()
                o, bias = mod[:, 4 * j:4 * j + 4], prm[:, PRM["b_ada"] + 4 * j:PRM["b_ada"] + 4 * j + 4]
                one = 1.0 if (4 * j) // KD in (1, 4) else 0.0
                MOD[j] = stt([t, SMALL], o, b.ap[:, 0:4], one, bias, ALU.add, ALU.add)
                b.free = [MOD[j]]
                return
            hi, lo, h, l = split_of[i]
            x, T = un["x"], un["T"]
            b, free = acc_banks.take()
            o = b.ap[:, 0:T]
            pe.wait([h, l] + free)
            for k in range(un["nk"]):
                pe.wait(x.ready[k])
                xh, xl = x.hi[:, k, x.base:x.base + T], x.lo[:, k, x.base:x.base + T]
                last = k == un["nk"] - 1
                parts = [mm(o, hi[:, k, :], xh, k == 0, False), mm(o, hi[:, k, :], xl, False, False),
                         mm(o, lo[:, k, :], xh, False, last)]
                if last:
                    t = pe.run([], *parts)
                else:
                    pe.steps.extend(parts)
            pe_of_unit[i] = t
            x.read = [t]
            b.free = un["evac"](un["n"], b.ap[:, 0:T], t)

        def fill(n):
            for _ in range(n):
                if taken[0] < stop_at[0]:
                    step()

        stop_at = [0]
        mark = {}

        def until(name):
            while taken[0] < mark[name]:
                step()

        def limit(name):
            stop_at[0] = mark[name]

        MOD = {}

        def part(at, n, w):
            return arena[:, at:at + n * w].rearrange("p (k t) -> p k t", t=w)

        o = 0
        qa = part(0, 24, SEQ)
        qb = part(6144, 8, SEQ)
        kb = part(8192, 8, SEQ)
        vbt = part(10240, 2, D)
        bias_b = part(12288, B_HEADS, SEQ)
        att_l = part(16384, 2, 384)
        att_p = part(17152, 2, 384)
        tmp_v = part(17920, 2, SEQ)
        zt = part(6144, 8, SEQ)
        gate = part(8192, 8, SEQ)
        merged = part(10240, 8, SEQ)
        DBUF = 12288

        def dbuf(i):
            return part(DBUF + 512 * i, 4, P)

        rows8 = part(18432, 5, SEQ)
        colq = small[:, 0:64].rearrange("p (q i) -> p q i", i=16)
        negmax = small[:, 64:80]
        rsum = small[:, 80:96]
        ea = small[:, 96:98]

        HB, HU = HIN, U
        HIN.base = 0
        W = ins["w_in"]
        qkv_a, z_a, q_b, gates = 0, 3 * D, 4 * D + 16, 7 * D + 16
        tiles_done = {}

        def keep(name, dst):
            def evac(n, ps, t):
                r = act.run([t] + tiles_done.get(name + "_free", []), lambda e: e.copy(dst[:, n, :], ps))
                tiles_done.setdefault(name, []).append(r)
                return [r]
            return evac

        def evac_rows(n, ps, t):
            r1 = act.run([t], lambda e: e.copy(rows8[0:8, 0, :], ps[0:8, :]))
            r2 = act.run([t], lambda e: e.copy(rows8[0:8, 1, :], ps[32:40, :]))
            tiles_done["rows"] = [r1, r2]
            return [r2]

        def evac_vb(n, ps, t):
            tmp = tmp_v[:, n % 2, :]
            r = act.run([t] + tiles_done.get(("vb", n - 2), []), lambda e: e.copy(tmp, ps))
            b, free = banks.take()
            tb = pe.run([r, SMALL] + free, *[tr(b.ap[:, a * P:(a + 1) * P], tmp[:, a * P:(a + 1) * P], P) for a in range(2)])
            tiles_done[("vb", n)] = [tb]
            w = dve.run([tb], lambda e: e.tensor_copy(vbt[:, :, n * P:(n + 1) * P],
                                                     b.ap[:, 0:2 * P].rearrange("p (a n) -> p a n", n=P)))
            b.free = [w]
            tiles_done.setdefault("vbt", []).append(w)
            return [r]

        def evac_conv_a(n, ps, t):
            y = qa[:, n, :]
            w = [prm_col("conv_a", j * 24 + n) for j in range(A_CONV)]
            r = act.run([t, SMALL], lambda e: e.activation(y, ps, ACT.Copy, scale=w[3]))
            for d in (1, 2, 3):
                r = stt([r, t], y[:, d:], ps[:, 0:SEQ - d], w[3 - d], y[:, d:], ALU.mult, ALU.add)
            tiles_done.setdefault("qa", []).append(r)
            return [r]

        def evac_gate(first):
            def evac(n, ps, t):
                g = gate[:, n, :]
                r = ts([t, SMALL] + tiles_done.get("gate_free", []), g, ps, prm_col("b_gate", first + n), ALU.add)
                fr = r
                r = fn([r], g, g, ACT.Exp, scale=-1.0)
                r = ts([r], g, g, 1.0, ALU.add)
                r = dve.run([r], lambda e: e.reciprocal(g, g))
                tiles_done[("gate", first + n)] = r
                return [fr]
            return evac

        def evac_branch_b(n, ps, t):
            r = tt([t, tiles_done[("gate", 8 + n)]], merged[:, n, :], ps, gate[:, n, :], ALU.mult)
            tiles_done[("merged", n)] = r
            tiles_done["gate_free"] = [r]
            return [r]

        def evac_branch_a(n, ps, t):
            g = gate[:, n, :]
            r = tt([t, tiles_done[("gate", n)]], g, ps, g, ALU.mult)
            m = tt([r, tiles_done[("merged", n)]], g, g, merged[:, n, :], ALU.add)
            split(MERGED, n, g, [m], SEQ)
            return [r]

        def split(x, k, src, after, T, free=()):
            hi, lo = x.hi[:, k, x.base:x.base + T], x.lo[:, k, x.base:x.base + T]
            h = act.run(list(after) + list(x.read) + list(free), lambda e: e.copy(hi, src))
            l = tt([h] + list(after) + list(x.read), lo, src, hi.bitcast(F32), ALU.subtract)
            x.ready[k] = [h, l]

        def evac_mix(n, ps, t):
            x = Xs[:, n, :]
            r = stt([t, XALPHA[0], MOD[4 + n // 4]], x, ps, mod[:, 2 * KD + n:2 * KD + n + 1], x, ALU.mult, ALU.add)
            XNEW[n] = r
            return [r]

        OB = Split(U.hi, U.lo)
        OA = Split(U.hi, U.lo)
        MERGED = Split(HIN.hi, HIN.lo)
        XNEW, XALPHA = {}, [None]

        for j in range(4):
            modulation(j)
        mark["start"] = len(units)
        weights(ins["w_thin"], (0, D), (0, P), HIN, SEQ, evac_rows, "rows")
        weights(W, (0, D), (q_b, q_b + D), HIN, SEQ, keep("qb", qb), "qb")
        weights(W, (0, D), (q_b + D, q_b + 2 * D), HIN, SEQ, keep("kb", kb), "kb")
        weights(W, (0, D), (q_b + 2 * D, q_b + 3 * D), HIN, SEQ, evac_vb, "vb")
        mark["vb"] = len(units)
        for j in range(4, 8):
            modulation(j)
        weights(W, (0, D), (qkv_a, qkv_a + 3 * D), HIN, SEQ, evac_conv_a, "qkv_a")
        mark["qkv_a"] = len(units)
        weights(W, (0, D), (z_a, z_a + D), HIN, SEQ, keep("z", zt), "z")
        mark["z"] = len(units)
        weights(W, (0, D), (gates + D, gates + 2 * D), HIN, SEQ, evac_gate(8), "gate_b")
        weights(ins["w_branch_b"], (0, D), (0, D), OB, SEQ, evac_branch_b, "branch_b")
        for j in range(8, 12):
            modulation(j)
        weights(W, (0, D), (gates, gates + D), HIN, SEQ, evac_gate(0), "gate_a")
        mark["gate_a"] = len(units)
        weights(ins["w_branch_a"], (0, D), (0, D), OA, SEQ, evac_branch_a, "branch_a")
        mark["branch_a"] = len(units)
        weights(ins["w_o"], (0, D), (0, D), MERGED, SEQ, evac_mix, "w_o")
        mark["w_o"] = len(units)

        sg = part(0, 8, LEN2)
        yv = part(8 * LEN2, 4, LEN2)
        RB = part(12 * LEN2, 1, LEN2)[:, 0, :]
        gtmp = part(13 * LEN2, 4, LEN2)
        sq = part(17 * LEN2, 8, LEN2)
        gla_at = 25 * LEN2
        RBT = {}

        def ffn_queue(w_up, w_down, x, T, gate_at, value_at, taps, bias, scaled, add, pre):
            state = {"y": 0, "free": {}}

            def conv(tile, ps, t, dst, free):
                w = [prm_col(taps, j * 2 * KF + tile) for j in range(3)]
                b = prm_col(bias, tile)
                src, done = ps, []
                if scaled:
                    i = state["y"] % 4
                    state["y"] += 1
                    src = gtmp[:, i, 0:T]
                    r0 = tt([t, RBT[pre]] + state["free"].get(("g", i), []), src, ps, RB[:, 0:T], ALU.mult)
                    done, t = [r0], r0
                r = fn([t] + free, dst, src, ACT.Identity, scale=w[2], bias=b)
                for d in (1, 2):
                    r = stt([r, t], dst[:, d:], src[:, 0:T - d], w[2 - d], dst[:, d:], ALU.mult, ALU.add)
                if scaled:
                    state["free"][("g", i)] = [r]
                return r, done or [r]

            for g in range(NG):
                k0, k1 = 8 * g, min(8 * g + 8, KF)

                def evac_gate_tile(n, ps, t, k0=k0, g=g):
                    dst = sg[:, n, 0:T]
                    r, done = conv(gate_at + k0 + n, ps, t, dst, state["free"].get(("sg", n), []))
                    state[("sg", n)] = fn([r], dst, dst, ACT.Silu)
                    return done

                def evac_value_tile(n, ps, t, k0=k0, g=g):
                    i = n % 4
                    y = yv[:, i, 0:T]
                    r, done = conv(value_at + k0 + n, ps, t, y, state["free"].get(("y", i), []))
                    m = tt([r, state[("sg", n)]], y, y, sg[:, n, 0:T], ALU.mult)
                    state["free"][("sg", n)] = [m]
                    split(UF, n, y, [m], T)
                    state["free"][("y", i)] = list(UF.ready[n])
                    return done

                def evac_down(n, ps, t, g=g):
                    return add(n, ps, t, g)

                weights(w_up, (0, D), ((gate_at + k0) * P, (gate_at + k1) * P), x, T, evac_gate_tile, "up_g")
                weights(w_up, (0, D), ((value_at + k0) * P, (value_at + k1) * P), x, T, evac_value_tile, "up_v")
                weights(w_down, (k0 * P, k1 * P), (0, D), UF, T, evac_down, "down")

        UF = Split(U.hi, U.lo)
        XF = {}

        def add_down_1(n, ps, t, g):
            x = Xs[:, n, :]
            XF[n] = stt([t, XF[n], MOD[10 + n // 4]], x, ps, mod[:, 5 * KD + n:5 * KD + n + 1], x, ALU.mult, ALU.add)
            return [XF[n]]

        def add_down_2(n, ps, t, g):
            x = X3[:, n, :]
            XF[n] = tt([t, XF[n]], x, ps, x, ALU.add)
            return [XF[n]]

        HF = Split(HIN.hi, HIN.lo)
        ffn_queue(ins["w_up"], ins["w_down"], HF, SEQ, 0, KF, "conv_f", "b_conv_f", False, add_down_1, "f")
        mark["ffn_first"] = len(units)

        G0 = gla_at
        fq, fk = part(G0, 4, LEN2), part(G0 + 1088, 4, LEN2)
        fvt = part(G0 + 2176, 3, 512)
        gq, gk = part(G0 + 3712, 2, LEN2), part(G0 + 4256, 2, LEN2)
        gvt = part(G0 + 4800, 3, 512)
        gkt = part(G0 + 6336, 3, 256)
        gr = part(G0 + 7104, 4, LEN2)
        la = part(G0 + 8192, 2, LEN2)
        lb = part(G0 + 8736, 2, LEN2)
        hist = part(G0 + 9280, 10, P)
        thin = part(G0 + 10560, 6, LEN2)
        assert G0 + 10560 + 6 * LEN2 <= NFA
        ot = part(0, 2, LEN2)
        fl = part(2 * LEN2, 2, 432)
        nb = part(2 * LEN2 + 864, 2, 432)
        fp = part(2 * LEN2 + 1728, 2, 3 * P)
        assert 2 * LEN2 + 1728 + 6 * P <= 12 * LEN2
        sqt, fs = sq[:, 0:2, :], sq[:, 2:4, :]

        B2 = {}

        def scaled_copy(name, dst, factor=None):
            def evac(n, ps, t):
                if factor is None:
                    r = tt([t, RBT["a"]], dst[:, n, :], ps, RB, ALU.mult)
                else:
                    r = stt([t, RBT["a"]], dst[:, n, :], ps, factor, RB, ALU.mult, ALU.mult)
                B2[(name, n)] = r
                return [r]
            return evac

        def evac_thin(n, ps, t):
            r1 = tt([t, RBT["a"]], thin[0:GLA_LOW, 0, :], ps[0:GLA_LOW, :], RB[0:GLA_LOW, :], ALU.mult)
            r2 = tt([t, RBT["a"]], thin[0:8, 1, :], ps[32:40, :], RB[32:40, :], ALU.mult)
            B2["thin"] = [r1, r2]
            return [r2]

        def to_tokens(name, dst):
            def evac(n, ps, t):
                i = n % 4
                tmp = gtmp[:, i, :]
                r = tt([t, RBT["a"]] + B2.get(("tmp", i), []), tmp, ps, RB, ALU.mult)
                b, free = banks.take()
                tb = pe.run([r] + free, *[tr(b.ap[0:w, j * P:(j + 1) * P], tmp[:, a:a + w], P)
                                          for j, (a, w) in enumerate(TOK2)])
                B2[("tmp", i)] = [tb]
                c1 = act.run([tb], lambda e: e.copy(dst[0:META, 0, n * P:(n + 1) * P], b.ap[0:META, 0:P]))
                c2 = act.run([tb], lambda e: e.copy(dst[:, 1:3, n * P:(n + 1) * P],
                                                    b.ap[:, P:3 * P].rearrange("p (a n) -> p a n", n=P)))
                b.free = [c2]
                B2[(name, n)] = c2
                return [r]
            return evac

        def evac_out(n, ps, t):
            x = X3[:, n, :]
            XF[n] = tt([t, XF[n]], x, ps, x, ALU.add)
            return [XF[n]]

        H2 = Split(HIN.hi, HIN.lo)
        O2 = Split(U.hi, U.lo)
        cuts = np.cumsum([0, 256, 256, 512, 512, GLA_LOW, 512, 512, 512, FOX_HEADS]).tolist()
        for l in range(LAYERS):
            w2 = ins["w_in_2"][l]
            weights(ins["w_thin"], (0, D), ((1 + l) * P, (2 + l) * P), H2, LEN2, evac_thin, "thin")
            mark[f"thin{l}"] = len(units)
            weights(w2, (0, D), (cuts[1], cuts[2]), H2, LEN2, scaled_copy("gk", gk), "gk")
            weights(w2, (0, D), (cuts[2], cuts[3]), H2, LEN2, to_tokens("gv", gvt), "gv")
            weights(w2, (0, D), (cuts[0], cuts[1]), H2, LEN2, scaled_copy("gq", gq, GLA_DK ** -0.5), "gq")
            mark[f"gla{l}"] = len(units)
            weights(w2, (0, D), (cuts[3], cuts[4]), H2, LEN2, scaled_copy("gr", gr), "gr")
            mark[f"gr{l}"] = len(units)
            weights(w2, (0, D), (cuts[5], cuts[6]), H2, LEN2, scaled_copy("fq", fq, FOX_DH ** -0.5), "fq")
            weights(w2, (0, D), (cuts[6], cuts[7]), H2, LEN2, scaled_copy("fk", fk), "fk")
            weights(w2, (0, D), (cuts[7], cuts[8]), H2, LEN2, to_tokens("fv", fvt), "fv")
            mark[f"fox{l}"] = len(units)
            weights(ins["w_out_2"][l], (0, D), (0, D), O2, LEN2, evac_out, "w_out")
            mark[f"w_out{l}"] = len(units)
            ffn_queue(ins["w_up_2"][l], ins["w_down_2"][l], H2, LEN2, KF, 0, f"conv_w{l}", f"conv_b{l}", True, add_down_2, "f")
            mark[f"ffn{l}"] = len(units)

        number_units()
        load_chunks()

        CACT = fn([SMALL], cact[:, :], prm[:, PRM["c"]:PRM["c"] + KD], ACT.Silu)
        until("start")
        htmp = part(0, 4, SEQ)
        for k in range(KD):
            d = htmp[:, k % 4, :]
            r = ts([SMALL, MOD[k // 4], MOD[2 + k // 4]] + (HIN.ready[k - 4] if k >= 4 else []), d, Xs[:, k, :],
                   mod[:, KD + k:KD + k + 1], ALU.mult, mod[:, k:k + 1], ALU.add)
            split(HIN, k, d, [r], SEQ)
            hlast = r
        XALPHA[0] = act.run([hlast], lambda e: e.mul(Xs, Xs, ALPHA))
        hin_split = HIN.ready[KD - 1]

        s_bias = sem("bias_loaded")
        rb = ins["rel_rev"]
        for p0, n in ((0, 256), (64, 192)):
            src = bass.AP(rb.tensor, 1 + p0, [[1, 64], [B_REL, B_HEADS], [1, n]])
            load(bias_b[p0:p0 + 64, :, 0:n], src, s_bias, hin_split)
        BMASK = dve.run(hin_split, lambda e: e.memset(bias_b[64:128, :, 192:256], NEG))
        for i in range(B_HEADS // 2):
            two = bias_b[:, 2 * i:2 * i + 2, :]
            b, free = banks.take()
            t = pe.run([(s_bias, 32), BMASK] + free, mm(b.ap[:, :], C("flip"), two))
            BIAS = act.run([t], lambda e, b=b, two=two: e.copy(two, b.ap[:, :].rearrange("p (h c) -> p h c", c=SEQ)))
            b.free = [BIAS]

        def delta_rows():
            R = [rows8[0:8, i, :] for i in range(5)]
            raw_t = tiles_done["rows"]
            r = fn(raw_t, R[0], R[0], ACT.Exp, scale=-1.0)
            r = ts([r], R[0], R[0], 1.0, ALU.add)
            beta = dve.run([r], lambda e: e.reciprocal(R[0], R[0]))
            x = ts(raw_t + [SMALL], R[1], R[1], prm8[0:8, 1:2], ALU.add)
            r = fn([x], R[2], R[1], ACT.Abs)
            r = fn([r], R[2], R[2], ACT.Exp, scale=-1.0)
            r = fn([r], R[2], R[2], ACT.Ln, bias=1.0)
            r = stt([r, x], R[1], R[1], 0.0, R[2], ALU.max, ALU.add)
            e_ = fn([SMALL], ea[0:8, 0:1], prm8[0:8, 0:1], ACT.Exp)
            r = ts([r, e_], R[1], R[1], ea[0:8, 0:1], ALU.mult, -1.0, ALU.mult)
            g = dve.run([r], lambda e: e.tensor_tensor_scan(R[3], C("restart", SEQ, rows=8), R[1], 0.0, ALU.mult, ALU.add))
            r = fn([g], R[4], R[3], ACT.Exp)
            beg = tt([r, beta], R[4], R[4], R[0], ALU.mult)
            g4 = R[3].rearrange("p (n c) -> p n c", c=CH)
            r = tt([g], R[2].rearrange("p (n c) -> p n c", c=CH),
                   g4[:, :, CH - 1:CH].broadcast_to([8, SEQ // CH, CH]), g4, ALU.subtract)
            egl = fn([r], R[2], R[2], ACT.Exp)
            b, free = banks.take()
            jobs = []
            for q, src in enumerate((R[3], R[0], R[4], R[2])):
                for t in range(2):
                    jobs.append(tr(b.ap[:, (q * 2 + t) * 8:(q * 2 + t) * 8 + 8], src[:, t * P:(t + 1) * P], 8))
            t_ = pe.run([g, beta, beg, egl, SMALL] + free, *jobs)
            cols = dve.run([t_], lambda e: e.tensor_copy(
                colq.rearrange("p q (h t) -> p q h t", t=2),
                b.ap[:, 0:64].rearrange("p (q t h) -> p q h t", q=4, t=2)))
            b.free = [cols]
            return cols, g

        until("vb")
        COLS, GROW = delta_rows()

        qk_ready = tiles_done["qb"] + tiles_done["kb"]
        l_free, p_free = [[], []], [[], []]
        out_bank = None

        def head_scores(h):
            j, r0 = h // 2, 64 * (h % 2)
            q, k = qb[r0:r0 + 64, j, :], kb[r0:r0 + 64, j, :]
            b, free = banks.take()
            t = pe.run(qk_ready + free, mm(b.ap[:, 0:P], q[:, 0:P], k[:, 0:P]),
                       mm(b.ap[:, P:3 * P], q[:, P:2 * P], k[:, 0:2 * P]))
            return b, t

        def head_softmax(h, b, t):
            L = att_l[:, h % 2, :]
            s1 = stt([t, BIAS] + l_free[h % 2], L[:, 0:P], b.ap[:, 0:P], B_DH ** -0.5, bias_b[:, h, P:2 * P], ALU.mult, ALU.add)
            s2 = stt([t], L[:, P:3 * P], b.ap[:, P:3 * P], B_DH ** -0.5, bias_b[:, h, :], ALU.mult, ALU.add)
            b.free = [s2]
            at = 4 * (h % 4)
            m = negmax[:, at:at + 2]
            m1 = dve.run([s1], lambda e: e.tensor_reduce(m[:, 0:1], L[:, 0:P], AX_X, ALU.max, negate=True))
            m2 = dve.run([s2], lambda e: e.tensor_reduce(m[:, 1:2], L[:, P:3 * P], AX_X, ALU.max, negate=True))
            rs = rsum[:, at:at + 2]
            e1 = fn([m1], L[:, 0:P], L[:, 0:P], ACT.Exp, bias=m[:, 0:1], accum_out=rs[:, 0:1])
            e2 = fn([m2], L[:, P:3 * P], L[:, P:3 * P], ACT.Exp, bias=m[:, 1:2], accum_out=rs[:, 1:2])
            rc = dve.run([e1, e2], lambda e: e.reciprocal(rs, rs))
            n1 = ts([rc], L[:, 0:P], L[:, 0:P], rs[:, 0:1], ALU.mult)
            n2 = ts([rc], L[:, P:3 * P], L[:, P:3 * P], rs[:, 1:2], ALU.mult)
            return [n1, n2]

        def head_values(h, norm):
            nonlocal out_bank
            L, PT = att_l[:, h % 2, :], att_p[:, h % 2, :]
            b, free = banks.take()
            t = pe.run(norm + free, *[tr(b.ap[:, a * P:(a + 1) * P], L[:, a * P:(a + 1) * P], P) for a in range(3)])
            l_free[h % 2] = [t]
            c = act.run([t] + p_free[h % 2], lambda e: e.copy(PT, b.ap[:, 0:3 * P]))
            b.free = [c]
            if h % 2 == 0:
                out_bank, ofree = banks.take()
            else:
                ofree = []
            r0 = 64 * (h % 2)
            o = out_bank.ap[r0:r0 + 64, :]
            v = vbt[:, :, h * 64:(h + 1) * 64]
            t = pe.run([c] + tiles_done["vbt"] + ofree, mm(o[:, 0:P], v[:, 0, :], PT[:, 0:P]),
                       mm(o[:, P:2 * P], v[:, 0, :], PT[:, P:2 * P], True, False),
                       mm(o[:, P:2 * P], v[:, 1, :], PT[:, 2 * P:3 * P], False, True))
            p_free[h % 2] = [t]
            if h % 2:
                split(OB, h // 2, out_bank.ap[:, 0:SEQ], [t], SEQ)
                out_bank.free = list(OB.ready[h // 2])

        limit("qkv_a")
        before = None
        for h in range(B_HEADS + 1):
            if h < B_HEADS:
                b, t = head_scores(h)
            fill(1)
            if h < B_HEADS:
                norm = head_softmax(h, b, t)
            if before is not None:
                head_values(h - 1, before)
            fill(1)
            before = norm
        until("qkv_a")

        tiles_done["z_free"] = p_free[0] + p_free[1]
        att_done = p_free[0] + p_free[1]
        QA = [fn([tiles_done["qa"][8 * a + 7]], qa[:, 8 * a:8 * a + 8, :], qa[:, 8 * a:8 * a + 8, :], ACT.Silu) for a in range(3)]
        until("z")
        ZS = fn([tiles_done["z"][-1]], zt, zt, ACT.Silu)

        limit("gate_a")
        tiles_done["gate_free"] = att_done
        out_scale = A_DK ** -0.5
        dfree = list(att_done)
        UP = {"prev": dfree}

        def b4(bank):
            return bank.ap[:, :].rearrange("p (i n) -> p i n", n=P)

        def delta_group(g):
            nonlocal dfree
            W0 = dfree
            h0 = 2 * g
            DL, DU, AM, XX, XT, WT, LM, QKT, WN, VB, KDEC, EG = [dbuf(i) for i in range(12)]
            q2, k2, v2 = (qa[:, 8 * a + h0:8 * a + h0 + 2, :] for a in range(3))
            flat = lambda x: x.rearrange("p i n -> p (i n)")
            tri = lambda x: flat(x).rearrange("p (h n) -> p h n", n=SEQ)

            normed = []
            for a, (x, tmp) in enumerate(((q2, tri(DL)), (k2, tri(DU)))):
                s = fn([QA[a]] + W0, tmp, x, ACT.Square)
                b, free = banks.take()
                t = pe.run([s] + free, mm(b.ap[:, :], C("ones"), tmp))
                l_ = fn([t], tmp, b.ap[:, :].rearrange("p (h n) -> p h n", n=SEQ), ACT.Ln, bias=EPS_L2)
                b.free = [l_]
                l_ = fn([l_], tmp, tmp, ACT.Exp, scale=-0.5)
                if a == 0:
                    normed.append(stt([l_], x, x, out_scale, tmp, ALU.mult, ALU.mult))
                else:
                    normed.append(tt([l_], x, x, tmp, ALU.mult))
            nq, nk = normed
            fill(1)
            gb, free = banks.take()
            t = pe.run([GROW, nk, nq] + free, *[mm(gb.ap[:, hh * SEQ:(hh + 1) * SEQ],
                                                    C("ident", 1, rows=8, at=h0 + hh).broadcast_to([8, P]), rows8[0:8, 3, :])
                                                 for hh in range(2)])
            gcol = bci(colq[:, 0, 4 * g:4 * g + 4], P)
            r = tt([t, COLS, nq], DL, bc(C("mask_low"), 4), b4(gb), ALU.subtract)
            r = tt([r], DL, DL, gcol, ALU.add)
            low = fn([r], DL, DL, ACT.Exp)
            r = tt([t, nk], DU, bc(C("mask_up"), 4), b4(gb), ALU.add)
            r = tt([r], DU, DU, gcol, ALU.subtract)
            up = fn([r], DU, DU, ACT.Exp)
            eg = fn([t] + W0, tri(EG), gb.ap[:, :].rearrange("p (h n) -> p h n", n=SEQ), ACT.Exp)
            gb.free = [eg, r]
            kk, free = banks.take()
            kt = [k2[:, i // 2, (i % 2) * P:(i % 2 + 1) * P] for i in range(4)]
            qt = [q2[:, i // 2, (i % 2) * P:(i % 2 + 1) * P] for i in range(4)]
            vt = [v2[:, i // 2, (i % 2) * P:(i % 2 + 1) * P] for i in range(4)]
            t = pe.run([nk] + free, *[mm(kk.ap[:, i * P:(i + 1) * P], kt[i], kt[i]) for i in range(4)])
            for i in range(4):
                r = stt([t, low], AM[:, i, :], kk.ap[:, i * P:(i + 1) * P], colq[:, 1, 4 * g + i:4 * g + i + 1], DL[:, i, :],
                        ALU.mult, ALU.mult)
            kk.free, am = [r], r
            qk, free = banks.take()
            t = pe.run([nq, nk] + free, *[mm(qk.ap[:, i * P:(i + 1) * P], kt[i], qt[i]) for i in range(4)])
            qkt = tt([t, up], QKT, b4(qk), DU, ALU.mult)
            qk.free = [qkt]
            qe = tt([eg, t], q2, q2, tri(EG), ALU.mult)
            fill(1)
            b, free = banks.take()
            t = pe.run([nk] + free, *[tr(b.ap[:, i * P:(i + 1) * P], kt[i], P) for i in range(4)])
            KBG = DU
            kbg = tt([t, qkt], KBG, b4(b), bci(colq[:, 2, 4 * g:4 * g + 4], P), ALU.mult)
            kdec = tt([t], KDEC, b4(b), bci(colq[:, 3, 4 * g:4 * g + 4], P), ALU.mult)
            b.free = [kdec]
            b, free = banks.take()
            t = pe.run([QA[2]] + free, *[tr(b.ap[:, i * P:(i + 1) * P], vt[i], P) for i in range(4)])
            vb = tt([t], VB, b4(b), bci(colq[:, 1, 4 * g:4 * g + 4], P), ALU.mult)
            b.free = [vb]

            lev = lambda l: bc(C("levels", P, at=l * P), 4)
            r = tt([am], LM, AM, lev(0), ALU.mult)
            x = tt([r], XX, bc(C("ident"), 4), LM, ALU.subtract)
            b, free = banks.take()
            t = pe.run([x] + free, *[tr(b.ap[:, i * P:(i + 1) * P], XX[:, i, :], P) for i in range(4)])
            xt_ = act.run([t], lambda e, b=b: e.copy(XT, b4(b)))
            b.free = [xt_]
            tw = None
            for l in range(1, 6):
                m = tt([am] + ([tw] if tw else []), LM, AM, lev(l), ALU.mult)
                b1, free = banks.take()
                tw = pe.run([m, xt_] + free, *[mm(b1.ap[:, i * P:(i + 1) * P], LM[:, i, :], XT[:, i, :]) for i in range(4)])
                w = act.run([tw], lambda e, b=b1: e.copy(WT, b4(b)))
                b1.free = [w]
                if l % 2:
                    fill(1)
                if l < 5:
                    b2, free = banks.take()
                    t2 = pe.run([w, x] + free, *[mm(b2.ap[:, i * P:(i + 1) * P], WT[:, i, :], XX[:, i, :]) for i in range(4)])
                b3, free = banks.take()
                t3_ = pe.run([w, x] + free, *[mm(b3.ap[:, i * P:(i + 1) * P], XX[:, i, :], WT[:, i, :]) for i in range(4)])
                if l < 5:
                    x = tt([t2, t3_], XX, XX, b4(b2), ALU.subtract)
                    b2.free = [x]
                xt_ = tt([t3_], XT, XT, b4(b3), ALU.subtract)
                b3.free = [xt_]
            fill(1)
            b, free = banks.take()
            t = pe.run([xt_, kbg] + free, *[mm(b.ap[:, i * P:(i + 1) * P], KBG[:, i, :], XT[:, i, :]) for i in range(4)])
            wn = act.run([t], lambda e, b=b: e.mul(WN, b4(b), -1.0))
            b.free = [wn]
            S, VN = XX, LM
            ob, ofree = banks.take()
            s_tok = None
            tv_prev = ofree
            for n in range(SEQ // CH):
                t_, r0 = n // 2, CH * (n % 2)
                rows = slice(r0, r0 + CH)
                vbk, free = banks.take()
                jobs = []
                for hh in range(2):
                    i = 2 * hh + t_
                    o = vbk.ap[rows, hh * P:(hh + 1) * P]
                    jobs.append(mm(o, XT[:, i, rows], VB[:, i, :], True, n == 0))
                    if n:
                        jobs.append(mm(o, WN[:, i, rows], S[:, hh, :], False, True))
                t = pe.run([xt_, vb, wn] + free + ([s_tok] if n else []), *jobs)
                vn = dve.run([t], lambda e, vbk=vbk, rows=rows: e.tensor_copy(
                    VN[rows, 0:2, :], vbk.ap[rows, 0:2 * P].rearrange("p (h n) -> p h n", n=P)))
                vbk.free = [vn]
                jobs = []
                for hh in range(2):
                    i = 2 * hh + t_
                    o = ob.ap[:, hh * SEQ + n * CH:hh * SEQ + (n + 1) * CH]
                    jobs.append(mm(o, VN[rows, hh, :], QKT[rows, i, rows], True, n == 0))
                    if n:
                        jobs.append(mm(o, S[:, hh, :], q2[:, hh, n * CH:(n + 1) * CH], False, True))
                t_o = pe.run([vn, qkt, qe] + tv_prev, *jobs)
                tv_prev = []
                if n < SEQ // CH - 1:
                    sbk, free = banks.take()
                    t = pe.run([kdec] + free, *[mm(sbk.ap[:, hh * P:(hh + 1) * P], KDEC[rows, 2 * hh + t_, :], VN[rows, hh, :])
                                                for hh in range(2)])
                    if n == 0:
                        s_tok = dve.run([t, t3_], lambda e, sbk=sbk: e.tensor_copy(
                            S[:, 0:2, :], sbk.ap[:, 0:2 * P].rearrange("p (h n) -> p h n", n=P)))
                    else:
                        for hh in range(2):
                            s_tok = stt([t, t_o, s_tok, eg], S[:, hh, :], S[:, hh, :], tri(EG)[:, hh, (n + 1) * CH - 1:(n + 1) * CH],
                                        sbk.ap[:, hh * P:(hh + 1) * P], ALU.mult, ALU.add)
                    sbk.free = [s_tok]
                    if n % 2 == 0:
                        fill(1)
            o3 = ob.ap[:, :].rearrange("p (h n) -> p h n", n=SEQ)
            SQ, OT = tri(WT), tri(DL)
            r = fn([t_o, wn], SQ, o3, ACT.Square)
            b, free = banks.take()
            t = pe.run([r] + free, mm(b.ap[:, :], C("ones"), SQ))
            r = fn([t], SQ, b.ap[:, :].rearrange("p (h n) -> p h n", n=SEQ), ACT.Ln, bias=EPS_RMS, scale=1.0 / A_DK)
            b.free = [r]
            r = fn([r], SQ, SQ, ACT.Exp, scale=-0.5)
            r = stt([r, t_o], OT, o3, prm_col("norm_a", 0), SQ, ALU.mult, ALU.mult)
            ob.free = [r]
            r = tt([r, ZS], OT, OT, zt[:, h0:h0 + 2, :], ALU.mult)
            oa_jobs.append((h0, OT, r))
            dfree = [t_o, r]
            fill(1)
            assert OB.read and taken[0] >= mark_branch_b
            for hh in range(2):
                split(OA, h0 + hh, OT[:, hh, :], [r], SEQ, free=OB.read)
            dfree = [t_o] + OA.ready[h0] + OA.ready[h0 + 1]

        def eps_col(i, v):
            dst = small[:, 100 + i:101 + i]
            return dst, dve.run([], lambda e: e.memset(dst, v))

        EPS_L2, t1 = eps_col(0, L2_EPS)
        EPS_RMS, t2 = eps_col(1, RMS_EPS)
        EPS_LN, t3e = eps_col(2, LN_EPS)
        act.wait([t1, t2, t3e])

        oa_jobs = []
        mark_branch_b = [i for i, un in enumerate(units) if un["tag"] == "branch_b"][-1] + 1
        while taken[0] < mark_branch_b:
            step()
        for g in range(4):
            delta_group(g)
        until("gate_a")
        until("branch_a")
        until("w_o")

        def layer_norm(gain, shift, after):
            b, free = banks.take()
            t = None
            pe.wait(free)
            for k in range(KD):
                t = pe.run([after[k]], mm(b.ap[:, 0:SEQ], C("ones"), Xs[:, k, :], k == 0, k == KD - 1))
            s2 = sq[:, :, 0:SEQ]
            parts = []
            for a in range(4):
                ks = slice(2 * a, 2 * a + 2)
                r = stt([t], Xs[:, ks, :], bc(b.ap[:, 0:SEQ], 2), -1.0 / D, Xs[:, ks, :], ALU.mult, ALU.add)
                parts.append((ks, r, fn([r], s2[:, ks, :], Xs[:, ks, :], ACT.Square)))
            b.free = [r]
            b, free = banks.take()
            pe.wait(free)
            for k in range(KD):
                t = pe.run([parts[k // 2][2]], mm(b.ap[:, 0:SEQ], C("ones"), s2[:, k, :], k == 0, k == KD - 1))
            v = gtmp[:, 0, 0:SEQ]
            r = fn([t], v, b.ap[:, 0:SEQ], ACT.Ln, bias=EPS_LN, scale=1.0 / D)
            b.free = [r]
            r = fn([r], v, v, ACT.Exp, scale=-0.5)
            res = {}
            for a in range(4):
                ks = slice(2 * a, 2 * a + 2)
                m = tt([r], Xs[:, ks, :], Xs[:, ks, :], bc(v, 2), ALU.mult)
                for k in (2 * a, 2 * a + 1):
                    res[k] = fn([m], Xs[:, k, :], Xs[:, k, :], ACT.Identity, scale=prm_col(gain, k), bias=prm_col(shift, k))
            return res

        X1 = layer_norm("ln1_g", "ln1_b", XNEW)
        for k in range(KD):
            d = htmp2[:, k % 4, :] if False else gtmp[:, k % 4, 0:SEQ]
            r = ts([X1[k], MOD[6 + k // 4], MOD[8 + k // 4]] + (HF.ready[k - 4] if k >= 4 else [X1[KD - 1]]), d, Xs[:, k, :],
                   mod[:, 4 * KD + k:4 * KD + k + 1], ALU.mult, mod[:, 3 * KD + k:3 * KD + k + 1], ALU.add)
            split(HF, k, d, [r], SEQ, free=MERGED.read)
            XF[k] = act.run([r], lambda e, k=k: e.mul(Xs[:, k, :], Xs[:, k, :], ALPHA))
        UF.read = OA.read
        until("ffn_first")
        X2 = layer_norm("ln2_g", "ln2_b", XF)
        for k in range(KD):
            XF[k] = X2[k]

        def rms_factor(name, before):
            b, free = banks.take()
            o = b.ap[:, 0:LEN2]
            pe.wait(free)
            for k in range(KD):
                s = fn([XF[k], SMALL] + before, sq[:, k, :], X3[:, k, :], ACT.Square)
                t = pe.run([s], mm(o, C("ones"), sq[:, k, :], k == 0, k == KD - 1))
            r = fn([t] + before, RB, o, ACT.Ln, bias=EPS_RMS, scale=1.0 / D)
            b.free = [r]
            RBT[name] = fn([r], RB, RB, ACT.Exp, scale=-0.5)

        def gained(name, free):
            for k in range(KD):
                i = k % 4
                d = yv[:, i, :]
                r = ts([XF[k], SMALL] + (H2.ready[k - 4] if k >= 4 else free), d, X3[:, k, :], prm_col(name, k), ALU.mult)
                split(H2, k, d, [r], LEN2, free=HF.read + free)

        def log_sigmoid(after, x, tmp):
            r = fn(after, tmp, x, ACT.Abs)
            r = fn([r], tmp, tmp, ACT.Exp, scale=-1.0)
            r = fn([r], tmp, tmp, ACT.Ln, bias=1.0)
            return stt([r] + list(after), x, x, 0.0, tmp, ALU.min, ALU.subtract)

        def forget_rows(l):
            x, tmp, c = (thin[0:8, i, :] for i in (1, 2, 3))
            r = ts(B2["thin"] + [SMALL], x, x, prm8[0:8, 2 + l:3 + l], ALU.add)
            r = log_sigmoid([r], x, tmp)
            c_ = dve.run([r], lambda e: e.tensor_tensor_scan(c, C("ones", LEN2, rows=8), x, 0.0, ALU.mult, ALU.add))
            b, free = banks.take()
            t = pe.run([c_] + free, *[tr(b.ap[0:w, j * 8:(j + 1) * 8], c[:, a:a + w], 8) for j, (a, w) in enumerate(TOK2)])
            r1 = dve.run([t], lambda e: e.tensor_copy(small[0:META, 104:112], b.ap[0:META, 0:8]))
            r2 = dve.run([t], lambda e: e.tensor_copy(small[:, 112:128], b.ap[:, 8:24]))
            b.free = [r2]
            return c_, [r1, r2]

        def gla_decays(l):
            glr = thin[0:GLA_LOW, 0, :]
            out_ = []
            for i in range(2):
                b, free = banks.take()
                t = pe.run(B2["thin"] + [SMALL] + free,
                           mm(b.ap[:, 0:LEN2], walpha[0:GLA_LOW, (2 * l + i) * P:(2 * l + i + 1) * P], glr))
                x = la[:, i, :]
                r = ts([t], x, b.ap[:, 0:LEN2], prm_col(f"b_alpha{l}", i), ALU.add)
                b.free = [r]
                r = log_sigmoid([r], x, lb[:, i, :])
                r = ts([r], x, x, 1.0 / GLA_TAU, ALU.mult)
                r = dve.run([r], lambda e, i=i, x=x: e.tensor_tensor_scan(lb[:, i, :], C("restart_gla", LEN2), x, 0.0, ALU.mult, ALU.add))
                B = lb[:, i, :]
                Bc, xc = (v[:, META:LEN2].rearrange("p (n c) -> p n c", c=CH) for v in (B, x))
                r1 = tt([r], x[:, 0:META], B[:, META - 1:META].broadcast_to([P, META]), B[:, 0:META], ALU.subtract)
                r2 = tt([r], xc, Bc[:, :, CH - 1:CH].broadcast_to([P, 4, CH]), Bc, ALU.subtract)
                k_ = fn([r1, r2], x, x, ACT.Exp)
                d_ = fn([r2], B, B, ACT.Exp)
                out_.append((k_, d_))
            return out_

        def gla(l, dec):
            SQ_ = gtmp
            r = None
            kd = []
            for i in range(2):
                kd.append(tt([dec[i][0], B2[("gk", i)]], gk[:, i, :], gk[:, i, :], la[:, i, :], ALU.mult))
                b, free = banks.take()
                t = pe.run([kd[i]] + free, *[tr(b.ap[0:w, j * P:(j + 1) * P], gk[:, i, a:a + w], P) for j, (a, w) in enumerate(TOK2)])
                c1 = act.run([t], lambda e, b=b, i=i: e.copy(gkt[0:META, 0, i * P:(i + 1) * P], b.ap[0:META, 0:P]))
                c2 = act.run([t], lambda e, b=b, i=i: e.copy(gkt[:, 1:3, i * P:(i + 1) * P], b.ap[:, P:3 * P].rearrange("p (a n) -> p a n", n=P)))
                b.free = [c2]
            fill(2)
            toks = [c1, c2] + [B2[("gv", n)] for n in range(4)]
            st = {}
            for c in range(5):
                j = 0 if c == 0 else 1 + (c - 1) // 2
                r0 = 0 if c == 0 else CH * ((c - 1) % 2)
                n = META if c == 0 else CH
                b, free = banks.take()
                jobs = []
                for h in range(GLA_HEADS):
                    i, o0 = h // 2, 64 * (h % 2)
                    jobs.append(mm(b.ap[o0:o0 + 64, i * P:(i + 1) * P], gkt[r0:r0 + n, j, h * 64:(h + 1) * 64],
                                   gvt[r0:r0 + n, j, h * P:(h + 1) * P]))
                t = pe.run(toks + free, *jobs)
                for i in range(2):
                    dst = hist[:, 2 * c + i, :]
                    if c == 0:
                        st[(c, i)] = dve.run([t] + HIST, lambda e, b=b, i=i, dst=dst: e.tensor_copy(dst, b.ap[:, i * P:(i + 1) * P]))
                    else:
                        e_ = META + c * CH - 1
                        st[(c, i)] = stt([t, st[(c - 1, i)], dec[i][1]], dst, hist[:, 2 * c - 2 + i, :], lb[:, i, e_:e_ + 1],
                                         b.ap[:, i * P:(i + 1) * P], ALU.mult, ALU.add)
                b.free = [st[(c, 1)]]
            fill(1)
            for h in range(GLA_HEADS):
                i, o0 = h // 2, 64 * (h % 2)
                b, free = banks.take()
                jobs = []
                for c in range(5):
                    a, n = (0, META) if c == 0 else (META + (c - 1) * CH, CH)
                    jobs.append(mm(b.ap[:, a:a + n], hist[o0:o0 + 64, 2 * c + i, :], gq[o0:o0 + 64, i, a:a + n]))
                t = pe.run([st[(4, 0)], st[(4, 1)], B2[("gq", i)]] + free, *jobs)
                HIST[:] = [t]
                norm_out(b, t, "ones", GLA_DV, f"gla_norm{l}", h, h, gr[:, h, :], [B2["gr"]])
                fill(1)

        HIST = []
        no = {"n": 0, "free": [[], []]}

        def norm_out(b, t, ones, width, gain, col, tile, gate_, gate_t):
            i = no["n"] % 2
            no["n"] += 1
            o, s = ot[:, i, :], sqt[:, i, :]
            r = fn([t] + no["free"][i], s, b.ap[:, 0:LEN2], ACT.Square)
            b2, free = banks.take()
            t2_ = pe.run([r] + free, mm(b2.ap[:, 0:LEN2], C(ones), s))
            r = fn([t2_], s, b2.ap[:, 0:LEN2], ACT.Ln, bias=EPS_RMS, scale=1.0 / width)
            b2.free = [r]
            r = fn([r], s, s, ACT.Exp, scale=-0.5)
            r = stt([r, t] + no["free"][i], o, b.ap[:, 0:LEN2], prm_col(gain, col), s, ALU.mult, ALU.mult)
            b.free = [r]
            if gate_ is not None:
                r = tt([r] + gate_t, o, o, gate_, ALU.mult)
            split(O2, tile, o, [r], LEN2, free=UF.read)
            no["free"][i] = O2.ready[tile]

        FM = C("fox_mask", LEN2)

        def fox_scores(h, crow):
            j, r0 = h // 2, 64 * (h % 2)
            q, k = fq[r0:r0 + 64, j, :], fk[r0:r0 + 64, j, :]
            b, free = banks.take()
            pieces = [(0, TOK2[2], LEN2), (LEN2, TOK2[1], META + P), (LEN2 + META + P, TOK2[0], META)]
            t = pe.run([B2[("fq", j)], B2[("fk", j)]] + free,
                       *[mm(b.ap[0:w, at:at + n], q[:, a:a + w], k[:, 0:n]) for at, (a, w), n in pieces])
            b2, free = banks.take()
            t2_ = pe.run([crow] + free, mm(b2.ap[:, 0:LEN2], C("ident", 1, rows=8, at=h).broadcast_to([8, P]), thin[0:8, 3, :]))
            N = nb[:, h % 2, :]
            free = NBF[h % 2]
            n1 = tt([t2_] + free, N[:, 0:LEN2], FM, b2.ap[:, 0:LEN2], ALU.subtract)
            n2 = tt([t2_] + free, N[:, LEN2:LEN2 + META + P], FM[:, P:LEN2], b2.ap[:, 0:META + P], ALU.subtract)
            n3 = tt([t2_] + free, N[0:META, 416:432], FM[0:META, META + P:META + P + META], b2.ap[0:META, 0:META], ALU.subtract)
            b2.free = [n3]
            return b, t, (n1, n2, n3)

        NBF = [[], []]
        LF, PF = [[], []], [[], []]

        def fox_softmax(h, b, t, ns, ccol):
            L, N = fl[:, h % 2, :], nb[:, h % 2, :]
            at = 4 * (h % 4)
            m, rs = negmax[:, at:at + 3], rsum[:, at:at + 3]
            ex, rc_after = [], []
            for p_, (a, n, w, tile) in enumerate(((0, LEN2, P, 2), (LEN2, META + P, P, 1), (416, META, META, 0))):
                cq = small[0:w, 104 + 8 * tile + h:105 + 8 * tile + h]
                s = stt([t, ns[p_]] + ccol + LF[h % 2], L[0:w, a:a + n], b.ap[0:w, a:a + n], cq, N[0:w, a:a + n], ALU.add, ALU.add)
                mx = dve.run([s], lambda e, p_=p_, a=a, n=n, w=w: e.tensor_reduce(m[0:w, p_:p_ + 1], L[0:w, a:a + n], AX_X, ALU.max, negate=True))
                ex.append(fn([mx], L[0:w, a:a + n], L[0:w, a:a + n], ACT.Exp, bias=m[0:w, p_:p_ + 1], accum_out=rs[0:w, p_:p_ + 1]))
            b.free, NBF[h % 2] = [s], [s]
            res = []
            for p_, (a, n, w) in enumerate(((0, LEN2, P), (LEN2, META + P, P), (416, META, META))):
                rc = dve.run([ex[p_]], lambda e, p_=p_, w=w: e.reciprocal(rs[0:w, p_:p_ + 1], rs[0:w, p_:p_ + 1]))
                res.append(ts([rc], L[0:w, a:a + n], L[0:w, a:a + n], rs[0:w, p_:p_ + 1], ALU.mult))
            return res

        fob = {}

        def fox_values(h, norm, l):
            L, PT = fl[:, h % 2, :], fp[:, h % 2, :]
            b, free = banks.take()
            b2, free2 = banks.take()
            t = pe.run(norm + free + free2,
                       tr(b.ap[:, 0:P], L[:, META:META + P], P), tr(b.ap[:, P:2 * P], L[:, META + P:LEN2], P),
                       tr(b.ap[:, 2 * P:3 * P], L[:, LEN2 + META:LEN2 + META + P], P),
                       tr(b2.ap[0:META, 0:P], L[:, 0:META], P), tr(b2.ap[0:META, P:2 * P], L[:, LEN2:LEN2 + META], P),
                       tr(b2.ap[0:META, 2 * P:2 * P + META], L[0:META, 416:432], META))
            LF[h % 2] = [t]
            PS = fs[:, h % 2, :]
            c1 = act.run([t] + PF[h % 2], lambda e: e.copy(PT[:, 0:3 * P], b.ap[:, 0:3 * P]))
            c2 = act.run([t] + PF[h % 2], lambda e: e.copy(PS[0:META, :], b2.ap[0:META, 0:2 * P + META]))
            b.free, b2.free = [c1], [c2]
            if h % 2 == 0:
                fob["b"], ofree = banks.take()
            else:
                ofree = []
            r0 = 64 * (h % 2)
            o = fob["b"].ap[r0:r0 + 64, :]
            v = [fvt[0:w, j, h * 64:(h + 1) * 64] for j, (a, w) in enumerate(TOK2)]
            oc, ob_, oa = o[:, META + P:LEN2], o[:, META:META + P], o[:, 0:META]
            t = pe.run([c1, c2] + [B2[("fv", n)] for n in range(4)] + ofree,
                       mm(oc, v[1], PT[:, 0:P], True, False), mm(oc, v[2], PT[:, P:2 * P], False, False),
                       mm(oc, v[0], PS[0:META, 0:P], False, True),
                       mm(ob_, v[1], PT[:, 2 * P:3 * P], True, False), mm(ob_, v[0], PS[0:META, P:2 * P], False, True),
                       mm(oa, v[0], PS[0:META, 2 * P:2 * P + META]))
            PF[h % 2] = [t]
            if h % 2:
                norm_out(fob["b"], t, "halves", FOX_DH, f"fox_norm{l}", h // 2, 4 + h // 2, None, [])

        for l in range(LAYERS):
            before = list(H2.read)
            rms_factor("a", before)
            gained(f"attn_norm{l}", before + [RBT["a"]])
            until(f"thin{l}")
            until(f"gla{l}")
            dec = gla_decays(l)
            crow, ccol = forget_rows(l)
            until(f"gr{l}")
            B2["gr"] = fn([B2[("gr", 3)]], gr, gr, ACT.Silu)
            limit(f"fox{l}")
            gla(l, dec)
            until(f"fox{l}")
            held = None
            for h in range(FOX_HEADS + 1):
                if h < FOX_HEADS:
                    b, t, ns = fox_scores(h, crow)
                    now = fox_softmax(h, b, t, ns, ccol)
                if held is not None:
                    fox_values(h - 1, held, l)
                held = now
            until(f"w_out{l}")
            rms_factor("f", list(O2.read))
            gained(f"ffn_norm{l}", [RBT["f"]])
            UF.read = list(O2.read)
            until(f"ffn{l}")

        rms_factor("o", list(H2.read))
        s_out = sem("written")
        o_dram = out.rearrange("p (k t) -> p k t", t=SEQ)
        RBs = RB[:, META:LEN2]
        for k in range(KD):
            r = stt([XF[k], RBT["o"]], Xs[:, k, :], Xs[:, k, :], prm_col("final_norm", k), RBs, ALU.mult, ALU.mult)
            load(o_dram[:, k, :], Xs[:, k, :], s_out, [r])
        sp.wait([(s_out, 16 * KD)])
        assert taken[0] == len(units) and loaded[0] == len(chunks)

        block = ctx.enter_context(nc.Block())

        @block.sync
        def _(e):
            sp.play(e)

        @block.tensor
        def _(e):
            pe.play(e)

        @block.scalar
        def _(e):
            act.play(e)

        @block.vector
        def _(e):
            dve.play(e)


def columns(a):
    a = np.asarray(a)
    return np.ascontiguousarray(a.reshape(-1, P).T)


def kernel(**inputs):
    import concourse.bacc as bacc
    from concourse.bass_utils import run_bass_kernel_spmd

    v = {k: np.asarray(a) for k, a in inputs.items()}
    prm = {"c": v["c"], "b_ada": v["b_ada"], "b_gate": v["b_gate"], "conv_a": v["conv_a"], "norm_a": v["norm_a"],
           "ln1_g": v["ln1_g"], "ln1_b": v["ln1_b"], "ln2_g": v["ln2_g"], "ln2_b": v["ln2_b"],
           "conv_f": v["conv_ffn"], "b_conv_f": v["b_conv_ffn"], "final_norm": v["final_norm_2"]}
    for l in range(LAYERS):
        prm.update({f"attn_norm{l}": v["attn_norm_2"][l], f"b_alpha{l}": v["b_alpha_2"][l], f"gla_norm{l}": v["gla_norm_2"][l],
                    f"fox_norm{l}": v["fox_norm_2"][l], f"ffn_norm{l}": v["ffn_norm_2"][l],
                    f"conv_w{l}": v["conv_w_2"][l], f"conv_b{l}": v["conv_b_2"][l]})
    thin = np.zeros((D, (1 + LAYERS) * P), np.float32)
    w_in = v["w_in"][0]
    thin[:, 0:8] = w_in[:, 4 * D:4 * D + 8]
    thin[:, 32:40] = w_in[:, 4 * D + 8:4 * D + 16]
    for l in range(LAYERS):
        w2 = v["w_in_2"][l]
        thin[:, (1 + l) * P:(1 + l) * P + GLA_LOW] = w2[:, 1536:1536 + GLA_LOW]
        thin[:, (1 + l) * P + 32:(1 + l) * P + 40] = w2[:, 3088:3096]
    as_tiles = lambda a: np.ascontiguousarray(a.T.reshape(KD, P, -1).transpose(1, 0, 2).reshape(P, -1))
    arrays = {
        "x": as_tiles(v["x"][0]), "meta": as_tiles(v["meta_tokens_2"]),
        "params": np.concatenate([columns(prm[name]) for name, _ in _PRM], axis=1), "consts": constants(),
        "params8": np.ascontiguousarray(np.stack([v["a_log"][0], v["dt_bias"][0], v["b_forget_2"][0], v["b_forget_2"][1]], axis=1)),
        "rel_rev": np.ascontiguousarray(v["rel_bias"][0][:, ::-1]), "w_thin": thin,
        "w_ada": v["w_ada"][0], "w_in": w_in, "w_branch_a": v["w_branch_a"][0], "w_branch_b": v["w_branch_b"][0],
        "w_o": v["w_o"][0], "w_up": v["w_up"][0], "w_down": v["w_down"][0],
        "w_in_2": v["w_in_2"], "w_alpha_up_2": v["w_alpha_up_2"], "w_out_2": v["w_out_2"], "w_up_2": v["w_up_2"],
        "w_down_2": v["w_down_2"],
    }
    nc = bacc.Bacc("TRN2", target_bir_lowering=False, num_devices=1)
    aps, fed = {}, {}
    for name, a in arrays.items():
        a = np.ascontiguousarray(a)
        fed[f"in_{name}"] = a
        aps[name] = nc.dram_tensor(f"in_{name}", a.shape, mybir.dt.from_np(a.dtype), kind="ExternalInput").ap()
    out = nc.dram_tensor("out_x", (P, KD * SEQ), F32, kind="ExternalOutput").ap()
    two_blocks(nc, aps, out)
    r = run_bass_kernel_spmd(nc, [fed], core_ids=[0])
    y = r.results[0]["out_x"]
    return np.ascontiguousarray(y.reshape(P, KD, SEQ).transpose(2, 1, 0).reshape(1, SEQ, D))
```

```python
from contextlib import ExitStack

import numpy as np
import concourse.bass as bass
from concourse import mybir

F32 = mybir.dt.float32
F32R = mybir.dt.float32r
ALU = mybir.AluOpType
ACT = mybir.ActivationFunctionType
AX_X = mybir.AxisListType.X

P = 128
D = 1024
KD = D // P
SEQ = 256
META = 16
LEN2 = META + SEQ
CH = 64
A_HEADS, A_DK, A_CONV = 8, 128, 4
B_HEADS, B_DH = 16, 64
B_REL = 320
D_FF = 2816
KF = D_FF // P
NG = 3
ALPHA = 2.0 ** 0.25
LN_EPS, RMS_EPS, L2_EPS = 1e-5, 1e-6, 1e-6
LAYERS = 2
GLA_HEADS, GLA_DK, GLA_DV, GLA_LOW, GLA_TAU = 4, 64, 128, 16, 16.0
FOX_HEADS, FOX_DH = 8, 64
NEG = -1e30
TOK2 = [(0, META), (META, P), (META + P, P)]

_PRM = [("c", KD), ("b_ada", 6 * KD), ("b_gate", 2 * KD), ("conv_a", A_CONV * 24), ("norm_a", 1),
        ("ln1_g", KD), ("ln1_b", KD), ("ln2_g", KD), ("ln2_b", KD), ("conv_f", 3 * 2 * KF), ("b_conv_f", 2 * KF)]
for _l in range(LAYERS):
    _PRM += [(f"attn_norm{_l}", KD), (f"b_alpha{_l}", 2), (f"gla_norm{_l}", 4), (f"fox_norm{_l}", 4),
             (f"ffn_norm{_l}", KD), (f"conv_w{_l}", 3 * 2 * KF), (f"conv_b{_l}", 2 * KF)]
_PRM += [("final_norm", KD)]
PRM, NPRM = {}, 0
for _name, _n in _PRM:
    PRM[_name] = NPRM
    NPRM += _n

_CST = [("ident", P), ("flip", P), ("ones", LEN2), ("mask_low", P), ("mask_up", P), ("levels", 6 * P), ("halves", P),
        ("fox_mask", LEN2), ("restart_gla", LEN2), ("restart", SEQ)]
CST, NCST = {}, 0
for _name, _n in _CST:
    CST[_name] = NCST
    NCST += _n


def constants():
    i, j = np.arange(P)[:, None], np.arange(P)[None, :]
    same = (i // CH) == (j // CH)
    levels = []
    for l in range(6):
        b = 1 << l
        levels.append(((i // (2 * b)) == (j // (2 * b))) & ((i // b) % 2 == 1) & ((j // b) % 2 == 0))
    k = np.arange(LEN2)[None, :]
    out = np.zeros((P, NCST), np.float32)

    def put(name, a):
        out[:, CST[name]:CST[name] + a.shape[1]] = a

    put("ident", np.eye(P))
    put("flip", np.eye(P)[::-1])
    put("ones", np.ones((P, LEN2)))
    put("mask_low", np.where(same & (j <= i), 0.0, NEG))
    put("mask_up", np.where(same & (i <= j), 0.0, NEG))
    put("levels", np.concatenate(levels, axis=1))
    put("halves", same)
    put("fox_mask", np.where(k - TOK2[2][0] <= i, 0.0, NEG))
    put("restart_gla", np.broadcast_to(~((k == 0) | ((k >= META) & ((k - META) % CH == 0))), (P, LEN2)))
    put("restart", np.broadcast_to(np.arange(SEQ)[None, :] % CH != 0, (P, SEQ)))
    return out


class Queue:

    def __init__(self, sem, serial):
        self.serial = serial
        self.sem, self.count, self.steps, self.seen = sem, 0, [], {}

    def wait(self, tokens):
        for sem, value in tokens:
            if value > self.seen.get(id(sem), 0):
                self.seen[id(sem)] = value
                self.steps.append(lambda e, s=sem, v=value: e.wait_ge(s, v))

    def run(self, after, *fns, loose=False):
        self.wait(after)
        if self.serial and not loose and self.count:
            self.wait([(self.sem, self.count)])
        for fn in fns[:-1]:
            self.steps.append(fn)
        self.count += 1
        self.steps.append(lambda e, f=fns[-1]: f(e).then_inc(self.sem, 1))
        return (self.sem, self.count)

    def play(self, engine):
        for step in self.steps:
            step(engine)


class Bank:

    def __init__(self, ap):
        self.ap, self.free = ap, []


class Banks:
    def __init__(self, aps):
        self.all, self.at = [Bank(a) for a in aps], -1

    def held(self, spare=0):
        return sum(b.free is not None for b in self.all) <= spare

    def take(self):
        for _ in self.all:
            self.at = (self.at + 1) % len(self.all)
            b = self.all[self.at]
            if b.free is not None:
                free, b.free = b.free, None
                return b, free
        raise RuntimeError("all banks are held")


class Split:

    def __init__(self, hi, lo, base=0):
        self.hi, self.lo, self.base = hi, lo, base
        self.ready, self.read = [[] for _ in range(KD)], []
        self.pending = 0


def two_blocks(nc, ins, out):
    ctx = ExitStack()
    with ctx:
        def sb(name, cols, dt=F32):
            return ctx.enter_context(nc.sbuf_tensor(name, [P, cols], dt))

        def sem(name):
            return ctx.enter_context(nc.semaphore(name))

        pe, sp = (Queue(sem(n), False) for n in ("pe_done", "sp_done"))
        act, dve, pool = (Queue(sem(n), True) for n in ("act_done", "dve_done", "pool_done"))

        NRAW, NUNIT = 3, 3
        raw = sb("raw_weights", NRAW * 4096)
        whi = sb("weights_hi", NUNIT * 1024, F32R)
        wlo = sb("weights_lo", NUNIT * 1024, F32R)
        hin_hi = sb("hin_hi", KD * LEN2, F32R)
        hin_lo = sb("hin_lo", KD * LEN2, F32R)
        u_hi = sb("u_hi", KD * LEN2, F32R)
        u_lo = sb("u_lo", KD * LEN2, F32R)
        xt = sb("residual", KD * LEN2)
        cst = sb("constants", NCST)
        prm = sb("parameters", NPRM)
        prm8 = sb("head_parameters", 4)
        walpha = sb("w_alpha", LAYERS * 2 * P)
        mod = sb("modulation", 6 * KD)
        cact = sb("c_act", KD)
        small = sb("small", 256)
        NFA = 19712
        arena = sb("arena", NFA)

        def t3(x, n, w=LEN2):
            return x[:, 0:n * w].rearrange("p (k t) -> p k t", t=w)

        X3 = t3(xt, KD)
        HIN = Split(t3(hin_hi, KD), t3(hin_lo, KD))
        U = Split(t3(u_hi, KD), t3(u_lo, KD))
        Xs = X3[:, :, META:LEN2]

        def C(name, n=None, rows=P, at=0):
            a = CST[name] + at
            return cst[0:rows, a:a + (n or P)]

        def prm_col(name, i, rows=P):
            a = PRM[name] + i
            return prm[0:rows, a:a + 1]

        acc_banks = Banks([ctx.enter_context(nc.psum_tensor(f"acc{i}", [P, 512], F32)) for i in range(3)])
        banks = Banks([ctx.enter_context(nc.psum_tensor(f"part{i}", [P, 512], F32)) for i in range(5)])

        def mm(o, l, r, start=True, stop=True):
            return lambda e: e.matmul(o, l, r, start=start, stop=stop)

        def tr(o, i, rows):
            return lambda e: e.transpose(o, i, C("ident", rows, rows=rows))

        def tt(after, o, a, b, op, on=None, loose=False):
            return (on or dve).run(after, lambda e: e.tensor_tensor(o, a, b, op), loose=loose)

        def ts(after, o, a, s1, op0, s2=None, op1=None, on=None, loose=False):
            if op1 is None:
                return (on or dve).run(after, lambda e: e.tensor_scalar(o, a, s1, None, op0), loose=loose)
            return (on or dve).run(after, lambda e: e.tensor_scalar(o, a, s1, s2, op0, op1), loose=loose)

        def stt(after, o, a, s, b, op0, op1, loose=False):
            return dve.run(after, lambda e: e.scalar_tensor_tensor(out=o, in0=a, scalar=s, in1=b, op0=op0, op1=op1), loose=loose)

        def fn(after, o, i, f, loose=False, **kw):
            return act.run(after, lambda e: e.activation(o, i, f, **kw), loose=loose)

        def table(name):
            act.steps.append(lambda e: e.preload_act_table_set(name))

        EXP_LN, SILU = "natural_log_exp_and_others", "silu_and_others"

        def bc(ap, n):
            return ap.unsqueeze(1).broadcast_to([ap.shape[0], n, ap.shape[1]])

        def bci(ap, n):
            return ap.unsqueeze(2).broadcast_to([ap.shape[0], ap.shape[1], n])

        s_small = sem("small_loaded")
        loads = [
            (Xs, ins["x"].rearrange("p (k t) -> p k t", t=SEQ)),
            (prm[:, :], ins["params"]), (cst[:, :], ins["consts"]),
            (prm8[0:8, :], ins["params8"]),
            (X3[:, :, 0:META], ins["meta"].rearrange("p (k t) -> p k t", t=META)),
            (walpha[0:GLA_LOW, :].rearrange("p (l n) -> p l n", l=LAYERS), ins["w_alpha_up_2"].rearrange("l p n -> p l n")),
        ]

        def load(dst, src, s, after=()):
            sp.wait(after)
            sp.steps.append(lambda e: e.dma_start(dst, src).then_inc(s, 16))

        for dst, src in loads:
            load(dst, src, s_small)
        SMALL = (s_small, 16 * len(loads))

        raw_sem = [sem(f"raw{i}_loaded") for i in range(NRAW)]
        chunks = []
        units = []
        loaded = [0]

        chunk_read = {}

        def load_chunks():
            while loaded[0] < len(chunks) and (loaded[0] < NRAW or loaded[0] - NRAW in chunk_read):
                c = loaded[0]
                loaded[0] += 1
                load(chunk_ap(c), chunks[c][0], raw_sem[c % NRAW], chunk_read.get(c - NRAW, []))

        def chunk_ap(c):
            src, nk, w = chunks[c]
            r = c % NRAW
            return raw[:, r * 4096:r * 4096 + nk * w].rearrange("p (k n) -> p k n", n=w)

        def chunk_ready(c):
            return (raw_sem[c % NRAW], 16 * (c // NRAW + 1))

        def weights(w, rows, cols, x, T, evac, tag, ada=()):
            (r0, r1), (c0, c1) = rows, cols
            n0 = 0
            for a in range(c0, c1, 512):
                width = min(512, c1 - a)
                nk = (r1 - r0) // P
                chunks.append((w[r0:r1, a:a + width].rearrange("(k p) n -> p k n", p=P), nk, width))
                for j in range(width // P):
                    units.append(dict(chunk=len(chunks) - 1, col=j, nk=nk, x=x, T=T, evac=evac, n=n0,
                                      last=j == width // P - 1, tag=tag))
                    n0 += 1
                if (a - c0) // 512 % 2 == 0 and (a - c0) // 1024 < len(ada):
                    modulation(ada[(a - c0) // 1024])

        def modulation(j):
            w = ins["w_ada"]
            chunks.append((w[:, 512 * j:512 * (j + 1)].rearrange("(k p) n -> p k n", p=P), KD, 512))
            units.append(dict(chunk=len(chunks) - 1, ada=j, tag="ada"))

        flight = []

        def advance():
            for job in list(flight):
                if next(job, "end") == "end":
                    flight.remove(job)

        def go(job):
            if next(job, "end") != "end":
                flight.append(job)

        def drain():
            rounds = 0
            while flight:
                advance()
                rounds += 1
                assert rounds < 1000

        def grab(spare=0):
            while banks.held(spare):
                yield
            return banks.take()

        split_of, taken = {}, [0]
        pe_of_unit = {}

        def split_unit(i):
            if i >= len(units) or i in split_of or "ada" in units[i]:
                return
            un = units[i]
            slot = un["slot"]
            src = chunk_ap(un["chunk"])[:, :, un["col"] * P:(un["col"] + 1) * P]
            n = un["nk"] * P
            hi = whi[:, slot * 1024:slot * 1024 + n].rearrange("p (k n) -> p k n", n=P)
            lo = wlo[:, slot * 1024:slot * 1024 + n].rearrange("p (k n) -> p k n", n=P)
            free = [pe_of_unit[un["before"]]] if un["before"] is not None else []
            h = act.run([chunk_ready(un["chunk"])] + free, lambda e: e.copy(hi, src), loose=True)
            l = dve.run([chunk_ready(un["chunk"]), h] + free,
                        lambda e: e.tensor_tensor(lo, src, hi.bitcast(F32), ALU.subtract), loose=True)
            split_of[i] = (hi, lo, h, l)
            if un["last"]:
                chunk_read[un["chunk"]] = [h, l]
                load_chunks()

        def number_units():
            seen = []
            for i, un in enumerate(units):
                if "ada" in un:
                    continue
                un["slot"] = len(seen) % NUNIT
                un["before"] = seen[len(seen) - NUNIT] if len(seen) >= NUNIT else None
                seen.append(i)

        ada_sums, ada_late = {}, []

        def ada_columns(j, c):
            w = chunk_ap(c)
            b, free = yield from grab()
            t = pe.run([ada_sums[j], SMALL] + free,
                       *[mm(b.ap[:, m:m + 1], w[:, 0, m * P:(m + 1) * P], C("ones", 1)) for m in range(4)])
            chunk_read[c] = [t]
            load_chunks()
            o, bias = mod[:, 4 * j:4 * j + 4], prm[:, PRM["b_ada"] + 4 * j:PRM["b_ada"] + 4 * j + 4]
            one = 1.0 if (4 * j) // KD in (1, 4) else 0.0
            yield
            MOD[j] = stt([t, SMALL], o, b.ap[:, 0:4], one, bias, ALU.add, ALU.add)
            b.free = [MOD[j]]

        def step():
            i = taken[0]
            taken[0] += 1
            un = units[i]
            for a in range(i, i + NUNIT if un.get("ada", KD) >= 4 else i):
                if a < len(units) and "ada" not in units[a] and (units[a]["before"] is None or units[a]["before"] < i):
                    split_unit(a)
            if "ada" in un:
                c, j = un["chunk"], un["ada"]
                w = chunk_ap(c)
                ck = lambda k: cact[:, k:k + 1]
                if j < 4:
                    r = ts([chunk_ready(c), CACT], w[:, 0, :], w[:, 0, :], ck(0), ALU.mult)
                    for k in range(1, KD):
                        r = stt([r], w[:, 0, :], w[:, k, :], ck(k), w[:, 0, :], ALU.mult, ALU.add)
                else:
                    after = [chunk_ready(c), CACT]
                    for k in range(KD):
                        r = pool.run(after, lambda e, k=k: e.tensor_scalar(w[:, k, :], w[:, k, :], ck(k), None, ALU.mult))
                        if k:
                            r = pool.run([r], lambda e, k=k: e.tensor_tensor(w[:, 0, :], w[:, 0, :], w[:, k, :], ALU.add))
                ada_sums[j] = r
                if j < 4:
                    go(ada_columns(j, c))
                    advance()
                else:
                    ada_late.append((j, c))
                return
            hi, lo, h, l = split_of[i]
            x, T = un["x"], un["T"]
            while x.pending or acc_banks.held():
                advance()
            b, free = acc_banks.take()
            o = b.ap[:, 0:T]
            pe.wait([h, l] + free)
            for k in range(un["nk"]):
                pe.wait(x.ready[k])
                xh, xl = x.hi[:, k, x.base:x.base + T], x.lo[:, k, x.base:x.base + T]
                last = k == un["nk"] - 1
                parts = [mm(o, hi[:, k, :], xh, k == 0, False), mm(o, hi[:, k, :], xl, False, False),
                         mm(o, lo[:, k, :], xh, False, last)]
                if last:
                    t = pe.run([], *parts)
                else:
                    pe.steps.extend(parts)
            pe_of_unit[i] = t
            x.read = [t]
            advance()
            for a in range(i + 1, i + 1 + NUNIT + 1):
                if a < len(units) and "ada" not in units[a] and units[a]["before"] is not None and units[a]["before"] <= i:
                    split_unit(a)
            go(un["evac"](un["n"], b, b.ap[:, 0:T], t))
            if ada_late and un["last"]:
                go(ada_columns(*ada_late.pop(0)))

        def weave(jobs, most, apart, period):
            jobs, mine, r, last = list(jobs), [], 0, None
            while jobs or mine:
                mine = [job for job in mine if job in flight]
                if jobs and len(mine) < most and (last is None or r - last >= apart(len(jobs))):
                    go(jobs[0])
                    mine.append(jobs.pop(0))
                    last = r
                if taken[0] < stop_at[0] and r % period() == 0:
                    step()
                else:
                    advance()
                r += 1
                assert r < 2000

        stop_at = [0]
        mark = {}

        def until(name):
            while taken[0] < mark[name]:
                step()
            drain()

        def limit(name):
            stop_at[0] = mark[name]

        MOD = {}

        def part(at, n, w):
            return arena[:, at:at + n * w].rearrange("p (k t) -> p k t", t=w)

        o = 0
        qa = part(0, 24, SEQ)
        qb = part(6144, 8, SEQ)
        kb = part(8192, 8, SEQ)
        vbt = part(10240, 2, D)
        bias_b = part(12288, B_HEADS, SEQ)
        NATT = 5
        att = part(16384, NATT, 384)
        tmp_v = part(17920, 2, SEQ)
        rows8 = part(18432, 5, SEQ)
        zt = part(6144, 8, SEQ)
        merged = part(8192, 8, SEQ)
        NDBUF = 9
        DBUF = 10240
        assert DBUF + 2 * NDBUF * 512 == 18432 + 4 * SEQ
        colq = small[:, 0:64].rearrange("p (q i) -> p q i", i=16)
        negmax = small[:, 64:80]
        rsum = small[:, 80:96]
        ea = small[:, 96:98]

        HIN.base = 0
        W = ins["w_in"]
        qkv_a, z_a, q_b, gates = 0, 3 * D, 4 * D + 16, 7 * D + 16
        tiles_done = {}

        def keep(name, dst):
            def evac(n, b, ps, t):
                r = act.run([t] + tiles_done.get(name + "_free", []), lambda e: e.copy(dst[:, n, :], ps), loose=True)
                tiles_done.setdefault(name, []).append(r)
                b.free = [r]
                yield
            return evac

        def evac_rows(n, b, ps, t):
            r1 = act.run([t], lambda e: e.copy(rows8[0:8, 0, :], ps[0:8, :]))
            r2 = act.run([t], lambda e: e.copy(rows8[0:8, 1, :], ps[32:40, :]))
            tiles_done["rows"] = [r1, r2]
            b.free = [r2]
            yield

        def evac_vb(n, ba, ps, t):
            tmp = tmp_v[:, n % 2, :]
            r = act.run([t] + tiles_done.get(("vb", n - 2), []), lambda e: e.copy(tmp, ps), loose=True)
            ba.free = [r]
            yield
            b, free = yield from grab()
            tb = pe.run([r, SMALL] + free, *[tr(b.ap[:, a * P:(a + 1) * P], tmp[:, a * P:(a + 1) * P], P) for a in range(2)])
            tiles_done[("vb", n)] = [tb]
            yield
            w = dve.run([tb], lambda e: e.tensor_copy(vbt[:, :, n * P:(n + 1) * P],
                                                     b.ap[:, 0:2 * P].rearrange("p (a n) -> p a n", n=P)), loose=True)
            b.free = [w]
            tiles_done.setdefault("vbt", []).append(w)

        def evac_conv_a(n, b, ps, t):
            y = qa[:, n, :]
            w = [prm_col("conv_a", j * 24 + n) for j in range(A_CONV)]
            r = act.run([t, SMALL], lambda e: e.activation(y, ps, ACT.Copy, scale=w[3]), loose=True)
            yield
            for d in (1, 2, 3):
                r = stt([r, t], y[:, d:], ps[:, 0:SEQ - d], w[3 - d], y[:, d:], ALU.mult, ALU.add, loose=True)
            tiles_done.setdefault("qa", []).append(r)
            b.free = [r]

        def gate_tile(n):
            return merged[:, n - 8, :] if n >= 8 else qa[:, n if n < 4 else n + 4, :]

        def evac_gate(first):
            def evac(n, b, ps, t):
                g = gate_tile(first + n)
                r = ts([t, SMALL] + tiles_done["gate_free"], g, ps, prm_col("b_gate", first + n), ALU.add)
                b.free = [r]
                yield
                r = fn([r], g, g, ACT.Exp, scale=-1.0, loose=True)
                yield
                r = ts([r], g, g, 1.0, ALU.add)
                tiles_done[("gate", first + n)] = dve.run([r], lambda e: e.reciprocal(g, g))
            return evac

        def evac_branch_b(n, b, ps, t):
            r = tt([t, tiles_done[("gate", 8 + n)]], merged[:, n, :], ps, merged[:, n, :], ALU.mult)
            tiles_done[("merged", n)] = r
            b.free = [r]
            yield

        def evac_branch_a(n, b, ps, t):
            MERGED.pending += 1
            g = gate_tile(n)
            r = tt([t, tiles_done[("gate", n)]], g, ps, g, ALU.mult)
            m = tt([r, tiles_done[("merged", n)]], g, g, merged[:, n, :], ALU.add)
            b.free = [r]
            yield
            split(MERGED, n, g, [m], SEQ)
            MERGED.pending -= 1

        def split(x, k, src, after, T, free=(), low=None):
            hi, lo = x.hi[:, k, x.base:x.base + T], x.lo[:, k, x.base:x.base + T]
            h = act.run(list(after) + list(x.read) + list(free), lambda e: e.copy(hi, src), loose=True)
            l = tt([h] + list(after) + list(x.read) + list(free), lo, src, hi.bitcast(F32), ALU.subtract, on=low or pool, loose=True)
            x.ready[k] = [h, l]

        stat = {}

        def add_up(k, src, after, w, square):
            s = src
            if square:
                s = sq[:, k, 0:w]
                after = [fn(after, s, src, ACT.Square, loose=True)]
                yield
            if k == 0:
                stat["bank"], free = yield from grab()
                after = after + free
            stat["t"] = pe.run(after, mm(stat["bank"].ap[:, 0:w], C("ones"), s, k == 0, k == KD - 1))

        def evac_mix(n, b, ps, t):
            x = Xs[:, n, :]
            r = stt([t, XALPHA[0], MOD[4 + n // 4]], x, ps, mod[:, 2 * KD + n:2 * KD + n + 1], x, ALU.mult, ALU.add)
            b.free = [r]
            yield
            yield from add_up(n, x, [r], SEQ, False)

        OB = Split(U.hi, U.lo)
        OA = Split(U.hi, U.lo)
        MERGED = Split(HIN.hi, HIN.lo)
        XALPHA = [None]

        for j in range(4):
            modulation(j)
        mark["start"] = len(units)
        weights(ins["w_thin"], (0, D), (0, P), HIN, SEQ, evac_rows, "rows")
        weights(W, (0, D), (q_b, q_b + D), HIN, SEQ, keep("qb", qb), "qb")
        weights(W, (0, D), (q_b + D, q_b + 2 * D), HIN, SEQ, keep("kb", kb), "kb")
        weights(W, (0, D), (q_b + 2 * D, q_b + 3 * D), HIN, SEQ, evac_vb, "vb", ada=[4])
        mark["vb"] = len(units)
        weights(W, (0, D), (qkv_a, qkv_a + 3 * D), HIN, SEQ, evac_conv_a, "qkv_a", ada=[5, 6, 7])
        mark["qkv_a"] = len(units)
        weights(W, (0, D), (z_a, z_a + D), HIN, SEQ, keep("z", zt), "z", ada=[8])
        mark["z"] = len(units)
        weights(W, (0, D), (gates + D, gates + 2 * D), HIN, SEQ, evac_gate(8), "gate_b", ada=[9])
        weights(ins["w_branch_b"], (0, D), (0, D), OB, SEQ, evac_branch_b, "branch_b", ada=[10])
        mark["branch_b"] = len(units)
        weights(W, (0, D), (gates, gates + D), HIN, SEQ, evac_gate(0), "gate_a", ada=[11])
        mark["gate_a"] = len(units)
        weights(ins["w_branch_a"], (0, D), (0, D), OA, SEQ, evac_branch_a, "branch_a")
        mark["branch_a"] = len(units)
        weights(ins["w_o"], (0, D), (0, D), MERGED, SEQ, evac_mix, "w_o")
        mark["w_o"] = len(units)

        sg = part(0, 8, LEN2)
        yv = part(8 * LEN2, 4, LEN2)
        RB = part(12 * LEN2, 1, LEN2)[:, 0, :]
        yw = part(13 * LEN2, 4, LEN2)
        gtmp = yw
        sq = part(17 * LEN2, 8, LEN2)
        gla_at = 25 * LEN2

        def ffn_queue(w_up, w_down, x, T, gate_at, value_at, taps, bias, add):
            state = {"free": {}}

            def conv(tile, b, ps, t, dst, free):
                w = [prm_col(taps, j * 2 * KF + tile) for j in range(3)]
                r = fn([t] + free, dst, ps, ACT.Identity, scale=w[2], bias=prm_col(bias, tile), loose=True)
                yield
                for d in (1, 2):
                    r = stt([r, t], dst[:, d:], ps[:, 0:T - d], w[2 - d], dst[:, d:], ALU.mult, ALU.add, loose=True)
                b.free = [r]
                yield
                return r

            for g in range(NG):
                k0, k1 = 8 * g, min(8 * g + 8, KF)

                def evac_gate_tile(n, b, ps, t, k0=k0, g=g):
                    dst = sg[:, n, 0:T]
                    r = yield from conv(gate_at + k0 + n, b, ps, t, dst, state["free"].get(("sg", n), []))
                    state[("sg", n)] = fn([r], dst, dst, ACT.Silu, loose=True)

                def evac_value_tile(n, b, ps, t, k0=k0, g=g):
                    UF.pending += 1
                    y = (yv if n < 4 else yw)[:, n % 4, 0:T]
                    r = yield from conv(value_at + k0 + n, b, ps, t, y, state["free"].get(("y", n), []))
                    m = tt([r, state[("sg", n)]], y, y, sg[:, n, 0:T], ALU.mult, on=pool, loose=True)
                    state["free"][("sg", n)] = [m]
                    yield
                    split(UF, n, y, [m], T)
                    state["free"][("y", n)] = list(UF.ready[n])
                    UF.pending -= 1

                def evac_down(n, b, ps, t, g=g):
                    return add(n, b, ps, t, g)

                g0 = 0
                if g > 0:
                    g0 = 4
                    weights(w_up, (0, D), ((gate_at + k0) * P, (gate_at + k0 + g0) * P), x, T, evac_gate_tile, "up_g")
                    back[0]()
                weights(w_up, (0, D), ((gate_at + k0 + g0) * P, (gate_at + k1) * P), x, T,
                        lambda n, b, ps, t, g0=g0, f=evac_gate_tile: f(n + g0, b, ps, t), "up_g")
                weights(w_up, (0, D), ((value_at + k0) * P, (value_at + k1) * P), x, T, evac_value_tile, "up_v")
                back = [lambda k0=k0, k1=k1, f=evac_down: weights(w_down, (k0 * P, k1 * P), (0, D), UF, T, f, "down")]
            back[0]()

        UF = Split(U.hi, U.lo)
        XF = {}

        def add_down_1(n, b, ps, t, g):
            x = Xs[:, n, :]
            XF[n] = stt([t, XF[n], MOD[10 + n // 4]], x, ps, mod[:, 5 * KD + n:5 * KD + n + 1], x, ALU.mult, ALU.add, loose=True)
            b.free = [XF[n]]
            yield
            if g == NG - 1:
                yield from add_up(n, x, [XF[n]], SEQ, False)

        def add_residual(n, b, ps, t, last):
            x = X3[:, n, :]
            XF[n] = tt([t, XF[n]], x, ps, x, ALU.add, loose=True)
            b.free = [XF[n]]
            yield
            if last:
                yield from add_up(n, x, [XF[n]], LEN2, True)

        def add_down_2(n, b, ps, t, g):
            return add_residual(n, b, ps, t, g == NG - 1)

        def evac_out(n, b, ps, t):
            return add_residual(n, b, ps, t, True)

        HF = Split(HIN.hi, HIN.lo)
        ffn_queue(ins["w_up"], ins["w_down"], HF, SEQ, 0, KF, "conv_f", "b_conv_f", add_down_1)
        mark["ffn_first"] = len(units)

        G0 = gla_at
        fq, fk = part(G0, 4, LEN2), part(G0 + 1088, 4, LEN2)
        fvt = part(G0 + 2176, 3, 512)
        gq, gk = part(G0 + 3712, 2, LEN2), part(G0 + 4256, 2, LEN2)
        gvt = part(G0 + 4800, 3, 512)
        gkt = part(G0 + 6336, 3, 256)
        gr = part(G0 + 7104, 4, LEN2)
        la = part(G0 + 8192, 2, LEN2)
        lb = part(G0 + 8736, 2, LEN2)
        hist = part(G0 + 9280, 10, P)
        thin = part(G0 + 10560, 6, LEN2)
        assert G0 + 10560 + 6 * LEN2 <= NFA
        NFOX, NOUT = 5, 3
        fl = part(0, NFOX, 432)
        assert NFOX * 432 <= 8 * LEN2
        ot, sqt = yv[:, 0:NOUT, :], sq[:, 0:NOUT, :]
        fs = sq[:, NOUT:NOUT + NFOX, :]

        B2 = {}

        def scaled_copy(name, dst, factor=1.0):
            def evac(n, b, ps, t):
                B2[(name, n)] = act.run([t], lambda e: e.mul(dst[:, n, :], ps, factor))
                b.free = [B2[(name, n)]]
                yield
            return evac

        def evac_thin(n, b, ps, t):
            r1 = act.run([t], lambda e: e.copy(thin[0:GLA_LOW, 0, :], ps[0:GLA_LOW, :]))
            r2 = act.run([t], lambda e: e.copy(thin[0:8, 1, :], ps[32:40, :]))
            B2["thin"] = [r1, r2]
            b.free = [r2]
            yield

        def to_tokens(name, dst):
            def evac(n, ba, ps, t):
                tmp = gtmp[:, n, :]
                r = act.run([t] + B2.get(("tmp", n), []), lambda e: e.copy(tmp, ps))
                ba.free = [r]
                yield
                b, free = yield from grab()
                tb = pe.run([r] + free, *[tr(b.ap[0:w, j * P:(j + 1) * P], tmp[:, a:a + w], P)
                                          for j, (a, w) in enumerate(TOK2)])
                B2[("tmp", n)] = [tb]
                yield
                c1 = act.run([tb], lambda e: e.copy(dst[0:META, 0, n * P:(n + 1) * P], b.ap[0:META, 0:P]))
                c2 = act.run([tb], lambda e: e.copy(dst[:, 1:3, n * P:(n + 1) * P],
                                                    b.ap[:, P:3 * P].rearrange("p (a n) -> p a n", n=P)))
                b.free = [c2]
                B2[(name, n)] = c2
            return evac

        H2 = Split(HIN.hi, HIN.lo)
        O2 = Split(U.hi, U.lo)
        cuts = np.cumsum([0, 256, 256, 512, 512, GLA_LOW, 512, 512, 512, FOX_HEADS]).tolist()
        for l in range(LAYERS):
            w2 = ins["w_in_2"][l]
            weights(ins["w_thin"], (0, D), ((1 + l) * P, (2 + l) * P), H2, LEN2, evac_thin, "thin")
            mark[f"thin{l}"] = len(units)
            weights(w2, (0, D), (cuts[5], cuts[6]), H2, LEN2, scaled_copy("fq", fq, FOX_DH ** -0.5), "fq")
            weights(w2, (0, D), (cuts[6], cuts[7]), H2, LEN2, scaled_copy("fk", fk), "fk")
            weights(w2, (0, D), (cuts[7], cuts[8]), H2, LEN2, to_tokens("fv", fvt), "fv")
            mark[f"fox{l}"] = len(units)
            weights(w2, (0, D), (cuts[1], cuts[2]), H2, LEN2, scaled_copy("gk", gk), "gk")
            weights(w2, (0, D), (cuts[2], cuts[3]), H2, LEN2, to_tokens("gv", gvt), "gv")
            weights(w2, (0, D), (cuts[0], cuts[1]), H2, LEN2, scaled_copy("gq", gq, GLA_DK ** -0.5), "gq")
            weights(w2, (0, D), (cuts[3], cuts[4]), H2, LEN2, scaled_copy("gr", gr), "gr")
            mark[f"gr{l}"] = len(units)
            weights(ins["w_out_2"][l], (0, D), (0, D), O2, LEN2, evac_out, "w_out")
            mark[f"w_out{l}"] = len(units)
            ffn_queue(ins["w_up_2"][l], ins["w_down_2"][l], H2, LEN2, KF, 0, f"conv_w{l}", f"conv_b{l}", add_down_2)
            mark[f"ffn{l}"] = len(units)

        number_units()
        load_chunks()

        table(SILU)
        CACT = fn([SMALL], cact[:, :], prm[:, PRM["c"]:PRM["c"] + KD], ACT.Silu)
        until("start")
        htmp = part(0, 4, SEQ)
        def operand(k, x, r, d, w, free=()):
            yield
            yield
            split(x, k, d, [r], w, free=free, low=dve if k % 2 else pool)

        for k in range(KD):
            d = htmp[:, k % 4, :]
            r = ts([SMALL, MOD[k // 4], MOD[2 + k // 4]] + (HIN.ready[k - 4] if k >= 4 else []), d, Xs[:, k, :],
                   mod[:, KD + k:KD + k + 1], ALU.mult, mod[:, k:k + 1], ALU.add)
            go(operand(k, HIN, r, d, SEQ))
            advance()
            hlast = r
        drain()
        XALPHA[0] = act.run([hlast], lambda e: e.mul(Xs, Xs, ALPHA))

        s_bias = sem("bias_loaded")
        rb = ins["rel_rev"]
        for p0, n in ((0, 256), (64, 192)):
            src = bass.AP(rb.tensor, 1 + p0, [[1, 64], [B_REL, B_HEADS], [1, n]])
            load(bias_b[p0:p0 + 64, :, 0:n], src, s_bias)
        BMASK = dve.run([], lambda e: e.memset(bias_b[64:128, :, 192:256], NEG))
        for i in range(B_HEADS // 2):
            two = bias_b[:, 2 * i:2 * i + 2, :]
            b, free = banks.take()
            t = pe.run([(s_bias, 32), BMASK] + free, mm(b.ap[:, :], C("flip"), two))
            BIAS = act.run([t], lambda e, b=b, two=two: e.copy(two, b.ap[:, :].rearrange("p (h c) -> p h c", c=SEQ)))
            b.free = [BIAS]

        table(EXP_LN)

        def delta_rows():
            R = [rows8[0:8, i, :] for i in range(5)]
            raw_t = tiles_done["rows"]
            yield
            r = fn(raw_t, R[0], R[0], ACT.Exp, scale=-1.0)
            yield
            r = ts([r], R[0], R[0], 1.0, ALU.add)
            beta = dve.run([r], lambda e: e.reciprocal(R[0], R[0]))
            x = ts(raw_t + [SMALL], R[1], R[1], prm8[0:8, 1:2], ALU.add)
            yield
            r = fn([x], R[2], R[1], ACT.Abs)
            r = fn([r], R[2], R[2], ACT.Exp, scale=-1.0)
            r = fn([r], R[2], R[2], ACT.Ln, bias=1.0)
            e_ = fn([SMALL], ea[0:8, 0:1], prm8[0:8, 0:1], ACT.Exp)
            yield
            r = stt([r, x], R[1], R[1], 0.0, R[2], ALU.max, ALU.add)
            r = ts([r, e_], R[1], R[1], ea[0:8, 0:1], ALU.mult, -1.0, ALU.mult)
            g = dve.run([r], lambda e: e.tensor_tensor_scan(R[4], C("restart", SEQ, rows=8), R[1], 0.0, ALU.mult, ALU.add))
            yield
            r = fn([g], R[3], R[4], ACT.Exp)
            yield
            beg = tt([r, beta], R[3], R[3], R[0], ALU.mult)
            g4 = R[4].rearrange("p (n c) -> p n c", c=CH)
            r = tt([g], R[2].rearrange("p (n c) -> p n c", c=CH),
                   g4[:, :, CH - 1:CH].broadcast_to([8, SEQ // CH, CH]), g4, ALU.subtract)
            yield
            egl = fn([r], R[2], R[2], ACT.Exp)
            yield
            b, free = yield from grab()
            jobs = []
            for q, src in enumerate((R[4], R[0], R[3], R[2])):
                for t in range(2):
                    jobs.append(tr(b.ap[:, (q * 2 + t) * 8:(q * 2 + t) * 8 + 8], src[:, t * P:(t + 1) * P], 8))
            t_ = pe.run([g, beta, beg, egl, SMALL] + free, *jobs)
            yield
            cols = dve.run([t_], lambda e: e.tensor_copy(
                colq.rearrange("p q (h t) -> p q h t", t=2),
                b.ap[:, 0:64].rearrange("p (q t h) -> p q h t", q=4, t=2)))
            b.free = [cols]
            tiles_done["gate_columns"], tiles_done["gate_row"] = cols, g

        until("vb")
        go(delta_rows())

        qk_ready = tiles_done["qb"] + tiles_done["kb"]
        l_free = [tiles_done[("vb", 6)] + tiles_done[("vb", 7)] for _ in range(NATT)]
        out_banks = {}

        def band_head(h):
            j, r0 = h // 2, 64 * (h % 2)
            q, k = qb[r0:r0 + 64, j, :], kb[r0:r0 + 64, j, :]
            L, m, rs = att[:, h % NATT, :], negmax[:, 2 * (h % 8):2 * (h % 8) + 2], rsum[:, 2 * (h % 8):2 * (h % 8) + 2]
            b, free = yield from grab()
            t = pe.run(qk_ready + free, mm(b.ap[:, 0:P], q[:, 0:P], k[:, 0:P]),
                       mm(b.ap[:, P:3 * P], q[:, P:2 * P], k[:, 0:2 * P]))
            if h == B_HEADS - 1:
                tiles_done["z_free"] = tiles_done["gate_free"] = [t]
                limit("z")
            yield
            s1 = stt([t, BIAS] + l_free[h % NATT], L[:, 0:P], b.ap[:, 0:P], B_DH ** -0.5, bias_b[:, h, P:2 * P], ALU.mult, ALU.add, loose=True)
            s2 = stt([t], L[:, P:3 * P], b.ap[:, P:3 * P], B_DH ** -0.5, bias_b[:, h, :], ALU.mult, ALU.add, loose=True)
            b.free = [s2]
            m1 = dve.run([s1], lambda e: e.tensor_reduce(m[:, 0:1], L[:, 0:P], AX_X, ALU.max, negate=True), loose=True)
            m2 = dve.run([s2], lambda e: e.tensor_reduce(m[:, 1:2], L[:, P:3 * P], AX_X, ALU.max, negate=True), loose=True)
            yield
            e1 = fn([m1], L[:, 0:P], L[:, 0:P], ACT.Exp, bias=m[:, 0:1], accum_out=rs[:, 0:1], loose=True)
            e2 = fn([m2], L[:, P:3 * P], L[:, P:3 * P], ACT.Exp, bias=m[:, 1:2], accum_out=rs[:, 1:2], loose=True)
            yield
            rc = dve.run([e1, e2], lambda e: e.reciprocal(rs, rs), loose=True)
            yield
            n1 = fn([rc], L[:, 0:P], L[:, 0:P], ACT.Copy, scale=rs[:, 0:1], loose=True)
            n2 = fn([rc], L[:, P:3 * P], L[:, P:3 * P], ACT.Copy, scale=rs[:, 1:2], loose=True)
            yield
            b, free = yield from grab()
            t = pe.run([n1, n2] + free, *[tr(b.ap[:, a * P:(a + 1) * P], L[:, a * P:(a + 1) * P], P) for a in range(3)])
            yield
            c = act.run([t], lambda e: e.copy(L, b.ap[:, 0:3 * P]), loose=True)
            b.free = [c]
            yield
            ofree = []
            if h % 2 == 0:
                out_banks[j], ofree = yield from grab(1)
            while j not in out_banks:
                yield
            ob = out_banks[j]
            o = ob.ap[r0:r0 + 64, :]
            v = vbt[:, :, h * 64:(h + 1) * 64]
            t = pe.run([c] + tiles_done["vbt"] + ofree, mm(o[:, 0:P], v[:, 0, :], L[:, 0:P]),
                       mm(o[:, P:2 * P], v[:, 0, :], L[:, P:2 * P], True, False),
                       mm(o[:, P:2 * P], v[:, 1, :], L[:, 2 * P:3 * P], False, True))
            l_free[h % NATT] = [t]
            if h % 2:
                yield
                split(OB, j, ob.ap[:, 0:SEQ], [t], SEQ, low=dve)
                ob.free = list(OB.ready[j])

        limit("qkv_a")
        weave([band_head(h) for h in range(B_HEADS)], NATT, lambda left: 1 + left % 2, lambda: 1)
        att_done = [t for f in l_free for t in f]
        COLS, GROW = tiles_done["gate_columns"], tiles_done["gate_row"]

        table(SILU)
        QA = [fn([tiles_done["qa"][8 * a + 7]], qa[:, 8 * a:8 * a + 8, :], qa[:, 8 * a:8 * a + 8, :], ACT.Silu) for a in range(3)]
        until("z")
        ZS = fn([tiles_done["z"][-1]], zt, zt, ACT.Silu)
        table(EXP_LN)

        out_scale = A_DK ** -0.5
        dfree = [att_done + [COLS], att_done + [COLS]]
        groups_done = []

        def b4(bank):
            return bank.ap[:, :].rearrange("p (i n) -> p i n", n=P)

        def four(b, left, right):
            return [mm(b.ap[:, i * P:(i + 1) * P], left(i), right(i)) for i in range(4)]

        def turned(b, src):
            return [tr(b.ap[:, i * P:(i + 1) * P], src(i), P) for i in range(4)]

        def delta_group(g):
            W0 = dfree[g % 2]
            h0 = 2 * g
            DL, DU, AM, XX, XT, WT, LM, QKT, EG = [part(DBUF + 512 * (NDBUF * (g % 2) + i), 4, P) for i in range(NDBUF)]
            q2, k2, v2 = (qa[:, 8 * a + h0:8 * a + h0 + 2, :] for a in range(3))
            tri = lambda x: x.rearrange("p i n -> p (i n)").rearrange("p (h n) -> p h n", n=SEQ)
            as_heads = lambda b: b.ap[:, :].rearrange("p (h n) -> p h n", n=SEQ)
            kt, qt, vt = ((lambda i, x=x: x[:, i // 2, (i % 2) * P:(i % 2 + 1) * P]) for x in (k2, q2, v2))
            col = lambda q: bci(colq[:, q, 4 * g:4 * g + 4], P)

            sq_ = [fn([QA[a]] + W0, tmp, x, ACT.Square, loose=True) for a, (x, tmp) in enumerate(((q2, tri(DL)), (k2, tri(DU))))]
            yield
            bq, free = yield from grab()
            tq = pe.run([sq_[0]] + free, mm(bq.ap[:, :], C("ones"), tri(DL)))
            bk, free = yield from grab()
            tk = pe.run([sq_[1]] + free, mm(bk.ap[:, :], C("ones"), tri(DU)))
            yield
            rs_ = []
            for t, b, tmp in ((tq, bq, tri(DL)), (tk, bk, tri(DU))):
                r = fn([t], tmp, as_heads(b), ACT.Ln, bias=EPS_L2, loose=True)
                b.free = [r]
                rs_.append(fn([r], tmp, tmp, ACT.Exp, scale=-0.5, loose=True))
            yield
            nq = stt([rs_[0]], q2, q2, out_scale, tri(DL), ALU.mult, ALU.mult, loose=True)
            nk = tt([rs_[1]], k2, k2, tri(DU), ALU.mult, loose=True)
            gb, free = yield from grab()
            tg = pe.run([GROW] + free, *[mm(gb.ap[:, hh * SEQ:(hh + 1) * SEQ],
                                            C("ident", 1, rows=8, at=h0 + hh).broadcast_to([8, P]), rows8[0:8, 4, :])
                                         for hh in range(2)])
            yield
            r = tt([tg, COLS, nq], DL, bc(C("mask_low"), 4), b4(gb), ALU.subtract, loose=True)
            low = tt([r], DL, DL, col(0), ALU.add, loose=True)
            r = tt([tg, nk], DU, bc(C("mask_up"), 4), b4(gb), ALU.add, loose=True)
            up = tt([r], DU, DU, col(0), ALU.subtract, loose=True)
            kk, free = yield from grab()
            tkk = pe.run([nk] + free, *four(kk, kt, kt))
            yield
            eg = fn([tg, up] + W0, tri(EG), as_heads(gb), ACT.Exp, loose=True)
            low = fn([low], DL, DL, ACT.Exp, loose=True)
            up = fn([up], DU, DU, ACT.Exp, loose=True)
            gb.free = [eg, up]
            qk, free = yield from grab()
            tqk = pe.run([nq, nk] + free, *four(qk, kt, qt))
            yield
            for i in range(4):
                am = stt([tkk, low], AM[:, i, :], kk.ap[:, i * P:(i + 1) * P], colq[:, 1, 4 * g + i:4 * g + i + 1], DL[:, i, :],
                         ALU.mult, ALU.mult, loose=True)
            kk.free = [am]
            lev = lambda l: bc(C("levels", P, at=l * P), 4)
            m = tt([am], LM, AM, lev(0), ALU.mult, loose=True)
            x = tt([m], XX, bc(C("ident"), 4), LM, ALU.subtract, loose=True)
            kb_, free = yield from grab()
            tkb = pe.run([nk] + free, *turned(kb_, kt))
            yield
            b, free = yield from grab()
            t = pe.run([x] + free, *turned(b, lambda i: XX[:, i, :]))
            m = tt([am, x], LM, AM, lev(1), ALU.mult, loose=True)
            qkt = tt([tqk, up], QKT, b4(qk), DU, ALU.mult, loose=True)
            qk.free = [qkt]
            KDEC, KBG = DL, DU
            kbg = tt([tkb, qkt], KBG, b4(kb_), col(2), ALU.mult, loose=True)
            kdec = tt([tkb, am], KDEC, b4(kb_), col(3), ALU.mult, loose=True)
            kb_.free = [kdec]
            qe = tt([eg, tqk], q2, q2, tri(EG), ALU.mult, on=pool, loose=True)
            yield
            xt_ = act.run([t], lambda e, b=b: e.copy(XT, b4(b)), loose=True)
            b.free = [xt_]
            yield
            for l in range(1, 6):
                b1, free = yield from grab()
                tw = pe.run([m, xt_] + free, *four(b1, lambda i: LM[:, i, :], lambda i: XT[:, i, :]))
                yield
                w = act.run([tw], lambda e, b=b1: e.copy(WT, b4(b)), loose=True)
                b1.free = [w]
                if l < 5:
                    m = tt([tw], LM, AM, lev(l + 1), ALU.mult, loose=True)
                yield
                b3, free = yield from grab()
                txt = pe.run([w, x] + free, *four(b3, lambda i: XX[:, i, :], lambda i: WT[:, i, :]))
                if l < 5:
                    b2, free = yield from grab()
                    tx = pe.run([w, x] + free, *four(b2, lambda i: WT[:, i, :], lambda i: XX[:, i, :]))
                yield
                xt_ = tt([txt], XT, XT, b4(b3), ALU.subtract, loose=True)
                b3.free = [xt_]
                if l < 5:
                    x = tt([tx, txt], XX, XX, b4(b2), ALU.subtract, loose=True)
                    b2.free = [x]
            VB, WN, S, VN = WT, AM, XX, LM
            bv, free = yield from grab()
            tv = pe.run([QA[2]] + free, *turned(bv, vt))
            bw, free = yield from grab()
            t = pe.run([xt_, kbg] + free, *four(bw, lambda i: KBG[:, i, :], lambda i: XT[:, i, :]))
            yield
            wn = act.run([t, m], lambda e, b=bw: e.mul(WN, b4(b), -1.0), loose=True)
            bw.free = [wn]
            vb = tt([tv, txt], VB, b4(bv), col(1), ALU.mult, loose=True)
            bv.free = [vb]
            yield
            ob, ofree = yield from grab(1)
            s_tok = []
            for n in range(SEQ // CH):
                t_, r0 = n // 2, CH * (n % 2)
                rows = slice(r0, r0 + CH)
                vbk, free = yield from grab()
                jobs = []
                for hh in range(2):
                    i = 2 * hh + t_
                    o = vbk.ap[rows, hh * P:(hh + 1) * P]
                    jobs.append(mm(o, XT[:, i, rows], VB[:, i, :], True, n == 0))
                    if n:
                        jobs.append(mm(o, WN[:, i, rows], S[:, hh, :], False, True))
                t = pe.run([xt_, vb, wn] + free + s_tok, *jobs)
                yield
                vn = dve.run([t, m], lambda e, vbk=vbk, rows=rows: e.tensor_copy(
                    VN[rows, 0:2, :], vbk.ap[rows, 0:2 * P].rearrange("p (h n) -> p h n", n=P)), loose=True)
                vbk.free = [vn]
                yield
                last = n == SEQ // CH - 1
                if not last:
                    sbk, free = yield from grab()
                    ts_ = pe.run([kdec, vn] + free, *[mm(sbk.ap[:, hh * P:(hh + 1) * P], KDEC[rows, 2 * hh + t_, :], VN[rows, hh, :])
                                                      for hh in range(2)])
                jobs = []
                for hh in range(2):
                    i = 2 * hh + t_
                    o = ob.ap[:, hh * SEQ + n * CH:hh * SEQ + (n + 1) * CH]
                    jobs.append(mm(o, VN[rows, hh, :], QKT[rows, i, rows], True, n == 0))
                    if n:
                        jobs.append(mm(o, S[:, hh, :], q2[:, hh, n * CH:(n + 1) * CH], False, True))
                t_o = pe.run([vn, qkt, qe] + ofree, *jobs)
                ofree = []
                yield
                if n == 0:
                    s_tok = [dve.run([ts_, txt], lambda e, sbk=sbk: e.tensor_copy(
                        S[:, 0:2, :], sbk.ap[:, 0:2 * P].rearrange("p (h n) -> p h n", n=P)), loose=True)]
                elif not last:
                    s_tok = [stt([ts_, t_o, eg] + s_tok, S[:, hh, :], S[:, hh, :], tri(EG)[:, hh, (n + 1) * CH - 1:(n + 1) * CH],
                                 sbk.ap[:, hh * P:(hh + 1) * P], ALU.mult, ALU.add, loose=True) for hh in range(2)]
                if not last:
                    sbk.free = list(s_tok)
            SQ, OT = tri(WT), tri(DL)
            r = fn([t_o], SQ, as_heads(ob), ACT.Square, loose=True)
            yield
            b, free = yield from grab()
            t = pe.run([r] + free, mm(b.ap[:, :], C("ones"), SQ))
            yield
            r = fn([t], SQ, as_heads(b), ACT.Ln, bias=EPS_RMS, scale=1.0 / A_DK, loose=True)
            b.free = [r]
            r = fn([r], SQ, SQ, ACT.Exp, scale=-0.5, loose=True)
            yield
            r = stt([r, t_o], OT, as_heads(ob), prm_col("norm_a", 0), SQ, ALU.mult, ALU.mult, loose=True)
            ob.free = [r]
            r = tt([r, ZS], OT, OT, zt[:, h0:h0 + 2, :], ALU.mult, on=pool, loose=True)
            while taken[0] < mark["branch_b"]:
                yield
            yield
            for hh in range(2):
                split(OA, h0 + hh, OT[:, hh, :], [r], SEQ, free=OB.read)
            dfree[g % 2] = OA.ready[h0] + OA.ready[h0 + 1]
            groups_done.append(g)
            if len(groups_done) == 2:
                tiles_done["gate_free"] = [t_o]
                limit("gate_a")

        def eps_col(i, v):
            dst = small[:, 100 + i:101 + i]
            return dst, dve.run([], lambda e: e.memset(dst, v))

        EPS_L2, t1 = eps_col(0, L2_EPS)
        EPS_RMS, t2 = eps_col(1, RMS_EPS)
        EPS_LN, t3e = eps_col(2, LN_EPS)
        act.wait([t1, t2, t3e])

        limit("branch_b")
        weave([delta_group(g) for g in range(A_HEADS // 2)], 2, lambda left: 2, lambda: 6 if len(groups_done) >= 2 else 3)
        until("branch_b")
        until("gate_a")
        until("branch_a")
        until("w_o")

        def layer_norm(gain, shift, squares=False):
            table(EXP_LN)
            b, t = stat["bank"], stat["t"]
            s2 = sq[:, :, 0:SEQ]
            parts = []
            for a in range(4):
                ks = slice(2 * a, 2 * a + 2)
                r = stt([t], Xs[:, ks, :], bc(b.ap[:, 0:SEQ], 2), -1.0 / D, Xs[:, ks, :], ALU.mult, ALU.add, loose=True)
                parts.append(fn([r], s2[:, ks, :], Xs[:, ks, :], ACT.Square, loose=True))
            b.free = [r]
            b, free = banks.take()
            for k in range(KD):
                t = pe.run([parts[k // 2]] + free, mm(b.ap[:, 0:SEQ], C("ones"), s2[:, k, :], k == 0, k == KD - 1))
            v = RB[:, 0:SEQ]
            r = fn([t], v, b.ap[:, 0:SEQ], ACT.Ln, bias=EPS_LN, scale=1.0 / D)
            b.free = [r]
            r = fn([r], v, v, ACT.Exp, scale=-0.5)
            res = {}
            for a in range(4):
                ks = slice(2 * a, 2 * a + 2)
                m = tt([r], Xs[:, ks, :], Xs[:, ks, :], bc(v, 2), ALU.mult, loose=True)
                for k in (2 * a, 2 * a + 1):
                    res[k] = fn([m], Xs[:, k, :], Xs[:, k, :], ACT.Identity, scale=prm_col(gain, k), bias=prm_col(shift, k), loose=True)
                    if squares:
                        go(add_up(k, X3[:, k, :], [res[k], SMALL], LEN2, True))
            return res

        X1 = layer_norm("ln1_g", "ln1_b")
        table(SILU)
        for k in range(KD):
            d = gtmp[:, k % 4, 0:SEQ]
            r = ts([X1[k], MOD[6 + k // 4], MOD[8 + k // 4]] + (HF.ready[k - 4] if k >= 4 else []), d, Xs[:, k, :],
                   mod[:, 4 * KD + k:4 * KD + k + 1], ALU.mult, mod[:, 3 * KD + k:3 * KD + k + 1], ALU.add)
            go(operand(k, HF, r, d, SEQ, MERGED.read))
            advance()
            XF[k] = act.run([r], lambda e, k=k: e.mul(Xs[:, k, :], Xs[:, k, :], ALPHA))
        drain()
        UF.read = OA.read
        until("ffn_first")
        XF.update(layer_norm("ln2_g", "ln2_b", squares=True))
        drain()

        def rms_factor():
            table(EXP_LN)
            b = stat["bank"]
            r = fn([stat["t"]], RB, b.ap[:, 0:LEN2], ACT.Ln, bias=EPS_RMS, scale=1.0 / D)
            b.free = [r]
            return fn([r], RB, RB, ACT.Exp, scale=-0.5)

        def rms_norm(gain, read):
            rb_ = rms_factor()
            for k in range(KD):
                d = yv[:, k % 4, :]
                r = stt([XF[k], rb_] + (H2.ready[k - 4] if k >= 4 else read), d, X3[:, k, :], prm_col(gain, k), RB, ALU.mult, ALU.mult, loose=True)
                go(operand(k, H2, r, d, LEN2, read))
                advance()
            drain()

        def log_sigmoid(after, x, tmp):
            r = fn(after, tmp, x, ACT.Abs, loose=True)
            r = fn([r], tmp, tmp, ACT.Exp, scale=-1.0, loose=True)
            r = fn([r], tmp, tmp, ACT.Ln, bias=1.0, loose=True)
            yield
            return stt([r] + list(after), x, x, 0.0, tmp, ALU.min, ALU.subtract, loose=True)

        def need(*keys):
            while not all(key in B2 for key in keys):
                yield

        def forget_rows(l):
            x, tmp, c, nc_ = (thin[0:8, i, :] for i in (1, 2, 3, 4))
            r = ts(B2["thin"] + [SMALL], x, x, prm8[0:8, 2 + l:3 + l], ALU.add, loose=True)
            yield
            r = yield from log_sigmoid([r], x, tmp)
            c_ = dve.run([r], lambda e: e.tensor_tensor_scan(c, C("ones", LEN2, rows=8), x, 0.0, ALU.mult, ALU.add), loose=True)
            B2["minus_c"] = ts([c_], nc_, c, -1.0, ALU.mult, loose=True)
            b, free = yield from grab()
            t = pe.run([c_] + free, *[tr(b.ap[0:w, j * 8:(j + 1) * 8], c[:, a:a + w], 8) for j, (a, w) in enumerate(TOK2)])
            yield
            r1 = dve.run([t], lambda e: e.tensor_copy(small[0:META, 104:112], b.ap[0:META, 0:8]), loose=True)
            r2 = dve.run([t], lambda e: e.tensor_copy(small[:, 112:128], b.ap[:, 8:24]), loose=True)
            b.free = [r2]
            B2["c_columns"] = [r1, r2]

        def gla_decays(l):
            glr = thin[0:GLA_LOW, 0, :]
            rs_ = []
            for i in range(2):
                b, free = yield from grab()
                t = pe.run(B2["thin"] + [SMALL] + free,
                           mm(b.ap[:, 0:LEN2], walpha[0:GLA_LOW, (2 * l + i) * P:(2 * l + i + 1) * P], glr))
                yield
                r = ts([t], la[:, i, :], b.ap[:, 0:LEN2], prm_col(f"b_alpha{l}", i), ALU.add, loose=True)
                b.free = [r]
                rs_.append(r)
            yield
            r = yield from log_sigmoid(rs_, la, lb)
            r = ts([r], la, la, 1.0 / GLA_TAU, ALU.mult, loose=True)
            for i in range(2):
                x, B = la[:, i, :], lb[:, i, :]
                s_ = dve.run([r], lambda e, x=x, B=B: e.tensor_tensor_scan(B, C("restart_gla", LEN2), x, 0.0, ALU.mult, ALU.add), loose=True)
                Bc, xc = (v[:, META:LEN2].rearrange("p (n c) -> p n c", c=CH) for v in (B, x))
                r1 = tt([s_], x[:, 0:META], B[:, META - 1:META].broadcast_to([P, META]), B[:, 0:META], ALU.subtract, loose=True)
                r2 = tt([s_], xc, Bc[:, :, CH - 1:CH].broadcast_to([P, 4, CH]), Bc, ALU.subtract, loose=True)
            yield
            B2["k_decay"] = fn([r1, r2], la, la, ACT.Exp, loose=True)
            B2["decay"] = fn([r1, r2], lb, lb, ACT.Exp, loose=True)

        def gla(l):
            yield from need("k_decay", ("gk", 0), ("gk", 1))
            kd = tt([B2["k_decay"], B2[("gk", 0)], B2[("gk", 1)]], gk, gk, la, ALU.mult, loose=True)
            yield
            copies = []
            for i in range(2):
                b, free = yield from grab()
                t = pe.run([kd] + free, *[tr(b.ap[0:w, j * P:(j + 1) * P], gk[:, i, a:a + w], P) for j, (a, w) in enumerate(TOK2)])
                yield
                c1 = act.run([t], lambda e, b=b, i=i: e.copy(gkt[0:META, 0, i * P:(i + 1) * P], b.ap[0:META, 0:P]), loose=True)
                c2 = act.run([t], lambda e, b=b, i=i: e.copy(gkt[:, 1:3, i * P:(i + 1) * P], b.ap[:, P:3 * P].rearrange("p (a n) -> p a n", n=P)), loose=True)
                b.free = [c1, c2]
                copies += [c1, c2]
            yield from need(*[("gv", n) for n in range(4)])
            toks = copies + [B2[("gv", n)] for n in range(4)]
            st, held = {}, None

            def states(c, b, t):
                for i in range(2):
                    dst = hist[:, 2 * c + i, :]
                    if c == 0:
                        st[(c, i)] = dve.run([t] + HIST, lambda e, dst=dst, i=i: e.tensor_copy(dst, b.ap[:, i * P:(i + 1) * P]), loose=True)
                    else:
                        e_ = META + c * CH - 1
                        st[(c, i)] = stt([t, st[(c - 1, i)], B2["decay"]] + HIST, dst, hist[:, 2 * c - 2 + i, :], lb[:, i, e_:e_ + 1],
                                         b.ap[:, i * P:(i + 1) * P], ALU.mult, ALU.add, loose=True)
                b.free = [st[(c, 1)]]

            for c in range(5):
                j = 0 if c == 0 else 1 + (c - 1) // 2
                r0 = 0 if c == 0 else CH * ((c - 1) % 2)
                n = META if c == 0 else CH
                b, free = yield from grab()
                jobs = []
                for h in range(GLA_HEADS):
                    i, o0 = h // 2, 64 * (h % 2)
                    jobs.append(mm(b.ap[o0:o0 + 64, i * P:(i + 1) * P], gkt[r0:r0 + n, j, h * 64:(h + 1) * 64],
                                   gvt[r0:r0 + n, j, h * P:(h + 1) * P]))
                t = pe.run(toks + free, *jobs)
                if held:
                    states(*held)
                held = (c, b, t)
                yield
            states(*held)
            yield from need(("gq", 0), ("gq", 1), *[("gr", n) for n in range(4)])
            table(SILU)
            gr_done = fn([B2[("gr", 3)]], gr, gr, ACT.Silu)
            table(EXP_LN)
            for h in range(GLA_HEADS):
                i, o0 = h // 2, 64 * (h % 2)
                b, free = yield from grab(2)
                jobs = []
                for c in range(5):
                    a, n = (0, META) if c == 0 else (META + (c - 1) * CH, CH)
                    jobs.append(mm(b.ap[:, a:a + n], hist[o0:o0 + 64, 2 * c + i, :], gq[o0:o0 + 64, i, a:a + n]))
                t = pe.run([st[(4, 0)], st[(4, 1)], B2[("gq", i)]] + free, *jobs)
                HIST[:] = [t]
                yield
                go(norm_out(b, t, "ones", GLA_DV, f"gla_norm{l}", h, h, gr[:, h, :], [gr_done]))

        HIST = []
        no = {"n": 0, "busy": [False] * NOUT, "free": [[] for _ in range(NOUT)]}

        def norm_out(b, t, ones, width, gain, col, tile, gate_, gate_t):
            i = no["n"] % NOUT
            no["n"] += 1
            while no["busy"][i]:
                yield
            no["busy"][i] = True
            o, s = ot[:, i, :], sqt[:, i, :]
            r = fn([t] + no["free"][i], s, b.ap[:, 0:LEN2], ACT.Square, loose=True)
            yield
            b2, free = yield from grab()
            t2_ = pe.run([r] + free, mm(b2.ap[:, 0:LEN2], C(ones), s))
            yield
            r = fn([t2_], s, b2.ap[:, 0:LEN2], ACT.Ln, bias=EPS_RMS, scale=1.0 / width, loose=True)
            b2.free = [r]
            r = fn([r], s, s, ACT.Exp, scale=-0.5, loose=True)
            yield
            r = stt([r, t] + no["free"][i], o, b.ap[:, 0:LEN2], prm_col(gain, col), s, ALU.mult, ALU.mult, loose=True)
            b.free = [r]
            if gate_ is not None:
                r = tt([r] + gate_t, o, o, gate_, ALU.mult, on=pool, loose=True)
            yield
            split(O2, tile, o, [r], LEN2, free=UF.read)
            no["free"][i], no["busy"][i] = O2.ready[tile], False

        FM = C("fox_mask", LEN2)
        LF = [[] for _ in range(NFOX)]
        fox_banks = {}

        def fox_head(h, l):
            j, r0 = h // 2, 64 * (h % 2)
            q, k = fq[r0:r0 + 64, j, :], fk[r0:r0 + 64, j, :]
            L, PS = fl[:, h % NFOX, :], fs[:, h % NFOX, :]
            at = 3 * (h % NFOX)
            m, rs = negmax[:, at:at + 3], rsum[:, at:at + 3]
            pieces = [(0, TOK2[2], LEN2, 2, 0), (LEN2, TOK2[1], META + P, 1, P), (LEN2 + META + P, TOK2[0], META, 0, META + P)]
            yield from need(("fq", j), ("fk", j), "minus_c")
            b, free = yield from grab()
            jobs = []
            for at_, (a, w), n, tile, mask_at in pieces:
                o = b.ap[0:w, at_:at_ + n]
                jobs += [mm(o, q[:, a:a + w], k[:, 0:n], True, False),
                         mm(o, C("ident", 1, rows=8, at=h).broadcast_to([8, w]), thin[0:8, 4, 0:n], False, True)]
            t = pe.run([B2[("fq", j)], B2[("fk", j)], B2["minus_c"]] + free, *jobs)
            yield
            yield from need("c_columns")
            mx = []
            for p_, (at_, (a, w), n, tile, mask_at) in enumerate(pieces):
                cq = small[0:w, 104 + 8 * tile + h:105 + 8 * tile + h]
                s_ = stt([t] + B2["c_columns"] + LF[h % NFOX], L[0:w, at_:at_ + n], b.ap[0:w, at_:at_ + n], cq, FM[0:w, mask_at:mask_at + n],
                         ALU.add, ALU.add, loose=True)
                mx.append(dve.run([s_], lambda e, p_=p_, at_=at_, n=n, w=w: e.tensor_reduce(
                    m[0:w, p_:p_ + 1], L[0:w, at_:at_ + n], AX_X, ALU.max, negate=True), loose=True))
            b.free = [s_]
            yield
            ex = [fn([mx[p_]], L[0:w, at_:at_ + n], L[0:w, at_:at_ + n], ACT.Exp, bias=m[0:w, p_:p_ + 1],
                     accum_out=rs[0:w, p_:p_ + 1], loose=True) for p_, (at_, (a, w), n, tile, mask_at) in enumerate(pieces)]
            yield
            rc = [dve.run([ex[0], ex[1]], lambda e: e.reciprocal(rs[:, 0:2], rs[:, 0:2]), loose=True),
                  dve.run([ex[2]], lambda e: e.reciprocal(rs[0:META, 2:3], rs[0:META, 2:3]), loose=True)]
            norm = [ts(rc, L[0:w, at_:at_ + n], L[0:w, at_:at_ + n], rs[0:w, p_:p_ + 1], ALU.mult, on=pool, loose=True)
                    for p_, (at_, (a, w), n, tile, mask_at) in enumerate(pieces)]
            yield
            b, free = yield from grab(1)
            b2, free2 = yield from grab()
            t = pe.run(norm + free + free2,
                       tr(b.ap[:, 0:P], L[:, META:META + P], P), tr(b.ap[:, P:2 * P], L[:, META + P:LEN2], P),
                       tr(b.ap[:, 2 * P:3 * P], L[:, LEN2 + META:LEN2 + META + P], P),
                       tr(b2.ap[0:META, 0:P], L[:, 0:META], P), tr(b2.ap[0:META, P:2 * P], L[:, LEN2:LEN2 + META], P),
                       tr(b2.ap[0:META, 2 * P:2 * P + META], L[0:META, 416:432], META))
            yield
            c1 = act.run([t], lambda e: e.copy(L[:, 0:3 * P], b.ap[:, 0:3 * P]), loose=True)
            c2 = act.run([t] + LF[h % NFOX], lambda e: e.copy(PS[0:META, :], b2.ap[0:META, 0:2 * P + META]), loose=True)
            b.free, b2.free = [c1], [c2]
            yield from need(*[("fv", n) for n in range(4)])
            yield
            ofree = []
            if h % 2 == 0:
                fox_banks[(l, j)], ofree = yield from grab(2)
            while (l, j) not in fox_banks:
                yield
            ob = fox_banks[(l, j)]
            o = ob.ap[r0:r0 + 64, :]
            v = [fvt[0:w, j_, h * 64:(h + 1) * 64] for j_, (a, w) in enumerate(TOK2)]
            oc, ob_, oa = o[:, META + P:LEN2], o[:, META:META + P], o[:, 0:META]
            t = pe.run([c1, c2] + [B2[("fv", n)] for n in range(4)] + ofree,
                       mm(oc, v[1], L[:, 0:P], True, False), mm(oc, v[2], L[:, P:2 * P], False, False),
                       mm(oc, v[0], PS[0:META, 0:P], False, True),
                       mm(ob_, v[1], L[:, 2 * P:3 * P], True, False), mm(ob_, v[0], PS[0:META, P:2 * P], False, True),
                       mm(oa, v[0], PS[0:META, 2 * P:2 * P + META]))
            LF[h % NFOX] = [t]
            if h % 2:
                yield
                go(norm_out(ob, t, "halves", FOX_DH, f"fox_norm{l}", j, 4 + j, None, []))

        for l in range(LAYERS):
            B2.clear()
            rms_norm(f"attn_norm{l}", HF.read + H2.read)
            until(f"thin{l}")
            go(forget_rows(l))
            go(gla_decays(l))
            while taken[0] < mark[f"fox{l}"]:
                step()
            go(gla(l))
            limit(f"gr{l}")
            weave([fox_head(h, l) for h in range(FOX_HEADS)], NFOX, lambda left: 1 + left % 2, lambda: 1)
            until(f"gr{l}")
            until(f"w_out{l}")
            rms_norm(f"ffn_norm{l}", list(O2.read))
            table(SILU)
            UF.read = list(O2.read)
            until(f"ffn{l}")

        rb_out = rms_factor()
        s_out = sem("written")
        o_dram = out.rearrange("p (k t) -> p k t", t=SEQ)
        RBs = RB[:, META:LEN2]
        for k in range(KD):
            r = stt([XF[k], rb_out], Xs[:, k, :], Xs[:, k, :], prm_col("final_norm", k), RBs, ALU.mult, ALU.mult)
            load(o_dram[:, k, :], Xs[:, k, :], s_out, [r])
        sp.wait([(s_out, 16 * KD)])
        assert taken[0] == len(units) and loaded[0] == len(chunks)

        block = ctx.enter_context(nc.Block())

        @block.sync
        def _(e):
            sp.play(e)

        @block.tensor
        def _(e):
            pe.play(e)

        @block.scalar
        def _(e):
            act.play(e)

        @block.gpsimd
        def _(e):
            pool.play(e)

        @block.vector
        def _(e):
            dve.play(e)


def columns(a):
    a = np.asarray(a)
    return np.ascontiguousarray(a.reshape(-1, P).T)


def kernel(**inputs):
    import concourse.bacc as bacc
    from concourse.bass_utils import run_bass_kernel_spmd

    v = {k: np.asarray(a) for k, a in inputs.items()}
    prm = {"c": v["c"], "b_ada": v["b_ada"], "b_gate": v["b_gate"], "conv_a": v["conv_a"], "norm_a": v["norm_a"],
           "ln1_g": v["ln1_g"], "ln1_b": v["ln1_b"], "ln2_g": v["ln2_g"], "ln2_b": v["ln2_b"],
           "conv_f": v["conv_ffn"], "b_conv_f": v["b_conv_ffn"], "final_norm": v["final_norm_2"]}
    for l in range(LAYERS):
        prm.update({f"attn_norm{l}": v["attn_norm_2"][l], f"b_alpha{l}": v["b_alpha_2"][l], f"gla_norm{l}": v["gla_norm_2"][l],
                    f"fox_norm{l}": v["fox_norm_2"][l], f"ffn_norm{l}": v["ffn_norm_2"][l],
                    f"conv_w{l}": v["conv_w_2"][l], f"conv_b{l}": v["conv_b_2"][l]})
    thin = np.zeros((D, (1 + LAYERS) * P), np.float32)
    w_in = v["w_in"][0]
    thin[:, 0:8] = w_in[:, 4 * D:4 * D + 8]
    thin[:, 32:40] = w_in[:, 4 * D + 8:4 * D + 16]
    for l in range(LAYERS):
        w2 = v["w_in_2"][l]
        thin[:, (1 + l) * P:(1 + l) * P + GLA_LOW] = w2[:, 1536:1536 + GLA_LOW]
        thin[:, (1 + l) * P + 32:(1 + l) * P + 40] = w2[:, 3088:3096]
    as_tiles = lambda a: np.ascontiguousarray(a.T.reshape(KD, P, -1).transpose(1, 0, 2).reshape(P, -1))
    arrays = {
        "x": as_tiles(v["x"][0]), "meta": as_tiles(v["meta_tokens_2"]),
        "params": np.concatenate([columns(prm[name]) for name, _ in _PRM], axis=1), "consts": constants(),
        "params8": np.ascontiguousarray(np.stack([v["a_log"][0], v["dt_bias"][0], v["b_forget_2"][0], v["b_forget_2"][1]], axis=1)),
        "rel_rev": np.ascontiguousarray(v["rel_bias"][0][:, ::-1]), "w_thin": thin,
        "w_ada": v["w_ada"][0], "w_in": w_in, "w_branch_a": v["w_branch_a"][0], "w_branch_b": v["w_branch_b"][0],
        "w_o": v["w_o"][0], "w_up": v["w_up"][0], "w_down": v["w_down"][0],
        "w_in_2": v["w_in_2"], "w_alpha_up_2": v["w_alpha_up_2"], "w_out_2": v["w_out_2"], "w_up_2": v["w_up_2"],
        "w_down_2": v["w_down_2"],
    }
    nc = bacc.Bacc("TRN2", target_bir_lowering=False, num_devices=1)
    aps, fed = {}, {}
    for name, a in arrays.items():
        a = np.ascontiguousarray(a)
        fed[f"in_{name}"] = a
        aps[name] = nc.dram_tensor(f"in_{name}", a.shape, mybir.dt.from_np(a.dtype), kind="ExternalInput").ap()
    out = nc.dram_tensor("out_x", (P, KD * SEQ), F32, kind="ExternalOutput").ap()
    two_blocks(nc, aps, out)
    r = run_bass_kernel_spmd(nc, [fed], core_ids=[0])
    y = r.results[0]["out_x"]
    return np.ascontiguousarray(y.reshape(P, KD, SEQ).transpose(2, 1, 0).reshape(1, SEQ, D))
```
